# Optimizing a Trainium2 kernel written in Bass

```python
import math
import jax, jax.numpy as jnp
from jax import lax
import numpy as np

D_MODEL = 1024
BATCH = 1
SEQ = 256
DEPTH = 2

HEAD_DIM = 64
Q_BLOCK = 128
A_HEADS = 4
A_QK = A_HEADS * 2 * HEAD_DIM
A_V = A_HEADS * 2 * HEAD_DIM
B_HEADS = 8
B_W = B_HEADS * HEAD_DIM
GRID_W = 64
NA_ROWS_MAX = 8
NA_COLS = 16
C_HEADS = 8
C_W = C_HEADS * HEAD_DIM
C_CONFIGS = ((128, 1), (512, 4), (2048, 16))
T5_BUCKETS = 32
T5_MAX_DIST = 1024
T5_HEADS = A_HEADS + C_HEADS
D_FF = 2816
N_BRANCH = 3
IN_SPLITS = [A_QK, A_QK, A_V, B_W, B_W, B_W, C_W, C_W, C_W]
IN_COLS = sum(IN_SPLITS) + N_BRANCH * D_MODEL
EPS = 1e-6

kernel_name = "hybrid_gated_diff_na_dilated_encoder"

def rmsnorm(x, g):
    xf = x.astype(jnp.float32)
    y = xf * lax.rsqrt(jnp.mean(xf * xf, axis=-1, keepdims=True) + EPS)
    return (y * g.astype(jnp.float32)).astype(x.dtype)

def swiglu(h, w1, w3, w2):
    return (jax.nn.silu(h @ w1) * (h @ w3)) @ w2

def t5_bucket(rel):
    nb = T5_BUCKETS // 2
    max_exact = nb // 2
    ret = jnp.where(rel > 0, nb, 0)
    n = jnp.abs(rel)
    nf = jnp.maximum(n, 1).astype(jnp.float32)
    large = max_exact + (jnp.log(nf / max_exact) / math.log(T5_MAX_DIST / max_exact)
                         * (nb - max_exact)).astype(jnp.int32)
    large = jnp.minimum(large, nb - 1)
    return ret + jnp.where(n < max_exact, n, large)

def diff_attention(q, k, v, bias_table, lam_full, subln_g, lam_init):
    B, S = q.shape[0], q.shape[1]
    nblk = S // Q_BLOCK
    scale = HEAD_DIM ** -0.5
    qb = (q * scale).reshape(B, nblk, Q_BLOCK, A_HEADS, 2, HEAD_DIM).transpose(1, 0, 3, 4, 2, 5)
    kt = k.transpose(0, 2, 3, 1, 4)
    vt = v.transpose(0, 2, 1, 3)
    kpos = jnp.arange(S)

    def block(args):
        qblk, i = args
        qpos = i * Q_BLOCK + jnp.arange(Q_BLOCK)
        bias = bias_table[t5_bucket(kpos[None, :] - qpos[:, None])].astype(jnp.float32)
        s = jnp.einsum('bhmqd,bhmkd->bhmqk', qblk, kt).astype(jnp.float32)
        s = s + bias.transpose(2, 0, 1)[None, :, None]
        pr = jax.nn.softmax(s, axis=-1)
        attn = pr[:, :, 0] - lam_full.astype(jnp.float32) * pr[:, :, 1]
        return jnp.einsum('bhqk,bhke->bhqe', attn.astype(v.dtype), vt)

    o = lax.map(block, (qb, jnp.arange(nblk)))
    o = o.transpose(1, 0, 3, 2, 4).reshape(B, S, A_HEADS, 2 * HEAD_DIM)
    o = rmsnorm(o, subln_g) * (1.0 - lam_init)
    return o.reshape(B, S, A_V)

def neighborhood_attention(q, k, v, rpb):
    B, S = q.shape[0], q.shape[1]
    rows = S // GRID_W
    kh = min(NA_ROWS_MAX, rows)
    kw = min(NA_COLS, GRID_W)
    scale = HEAD_DIM ** -0.5
    grid = lambda t: t.reshape(B, rows, GRID_W, B_HEADS, HEAD_DIM)
    qg = (grid(q) * scale).transpose(1, 0, 3, 2, 4)
    kg = grid(k).transpose(0, 3, 1, 2, 4)
    vg = grid(v).transpose(0, 3, 1, 2, 4)
    col = jnp.arange(GRID_W)
    cstart = jnp.clip(col - kw // 2, 0, GRID_W - kw)
    cidx = cstart[:, None] + jnp.arange(kw)[None, :]
    rel_c = cidx - col[:, None] + (NA_COLS - 1)

    def row_block(args):
        qrow, i = args
        rstart = jnp.clip(i - kh // 2, 0, rows - kh)
        krow = lax.dynamic_slice_in_dim(kg, rstart, kh, axis=2)
        vrow = lax.dynamic_slice_in_dim(vg, rstart, kh, axis=2)
        knb = krow[:, :, :, cidx]
        vnb = vrow[:, :, :, cidx]
        rel_r = rstart + jnp.arange(kh) - i + (NA_ROWS_MAX - 1)
        bias = rpb[:, rel_r[:, None, None], rel_c[None]].astype(jnp.float32)
        s = jnp.einsum('bhqd,bhrqcd->bhqrc', qrow, knb).astype(jnp.float32)
        s = s + bias.transpose(0, 2, 1, 3)[None]
        pr = jax.nn.softmax(s.reshape(B, B_HEADS, GRID_W, kh * kw), axis=-1)
        pr = pr.reshape(B, B_HEADS, GRID_W, kh, kw)
        return jnp.einsum('bhqrc,bhrqcd->bhqd', pr.astype(v.dtype), vnb)

    o = lax.map(row_block, (qg, jnp.arange(rows)))
    return o.transpose(1, 0, 3, 2, 4).reshape(B, S, B_W)

def dilated_attention(q, k, v, bias_table):
    B, S = q.shape[0], q.shape[1]
    nblk = S // Q_BLOCK
    scale = HEAD_DIM ** -0.5
    qb = (q * scale).reshape(B, nblk, Q_BLOCK, C_HEADS, HEAD_DIM).transpose(1, 0, 3, 2, 4)
    kt = k.transpose(0, 2, 1, 3)
    vt = v.transpose(0, 2, 1, 3)
    cfgs = [(w // (2 * r), r) for (w, r) in C_CONFIGS]
    max_pad = max(hf * r for (hf, r) in cfgs)
    kp = jnp.pad(kt, ((0, 0), (0, 0), (max_pad, max_pad), (0, 0)))
    vp = jnp.pad(vt, ((0, 0), (0, 0), (max_pad, max_pad), (0, 0)))

    def block(args):
        qblk, i = args
        qpos = i * Q_BLOCK + jnp.arange(Q_BLOCK)
        outs, lses = [], []
        for half, r in cfgs:
            offs = r * jnp.arange(-half, half + 1)
            kpos = qpos[:, None] + offs[None, :]
            valid = (kpos >= 0) & (kpos < S)
            kgat = kp[:, :, kpos + max_pad]
            vgat = vp[:, :, kpos + max_pad]
            bias = bias_table[t5_bucket(offs)].astype(jnp.float32)
            s = jnp.einsum('bhqd,bhqjd->bhqj', qblk, kgat).astype(jnp.float32)
            s = jnp.where(valid[None, None], s + bias.T[None, :, None, :], -jnp.inf)
            m = jnp.max(s, axis=-1, keepdims=True)
            e = jnp.exp(s - m)
            den = jnp.sum(e, axis=-1, keepdims=True)
            outs.append(jnp.einsum('bhqj,bhqjd->bhqd', (e / den).astype(v.dtype), vgat))
            lses.append(m + jnp.log(den))
        wts = jax.nn.softmax(jnp.concatenate(lses, axis=-1), axis=-1)
        return jnp.einsum('bhqn,nbhqd->bhqd', wts.astype(v.dtype), jnp.stack(outs))

    o = lax.map(block, (qb, jnp.arange(nblk)))
    return o.transpose(1, 0, 3, 2, 4).reshape(B, S, C_W)

def setup_inputs(seed: int = 0) -> dict:
    key = jax.random.key(seed)
    ks = jax.random.split(key, 26)
    nrm = lambda k, shape, s: jax.random.normal(k, shape, jnp.float32) * s
    gain = lambda k, shape: 1.0 + 0.05 * jax.random.normal(k, shape, jnp.float32)
    D = D_MODEL
    return {
        "x": nrm(ks[0], (BATCH, SEQ, D), 1.0),
        "g_ff1": gain(ks[1], (DEPTH, D)),
        "w1_ff1": nrm(ks[2], (DEPTH, D, D_FF), D ** -0.5),
        "w3_ff1": nrm(ks[3], (DEPTH, D, D_FF), D ** -0.5),
        "w2_ff1": nrm(ks[4], (DEPTH, D_FF, D), D_FF ** -0.5),
        "g_mix": gain(ks[5], (DEPTH, D)),
        "w_in": nrm(ks[6], (DEPTH, D, IN_COLS), D ** -0.5),
        "lam_q1": nrm(ks[7], (DEPTH, HEAD_DIM), 0.1),
        "lam_k1": nrm(ks[8], (DEPTH, HEAD_DIM), 0.1),
        "lam_q2": nrm(ks[9], (DEPTH, HEAD_DIM), 0.1),
        "lam_k2": nrm(ks[10], (DEPTH, HEAD_DIM), 0.1),
        "subln_g": gain(ks[11], (DEPTH, 2 * HEAD_DIM)),
        "na_rpb": nrm(ks[12], (DEPTH, B_HEADS, 2 * NA_ROWS_MAX - 1, 2 * NA_COLS - 1), 0.5),
        "t5_table": nrm(ks[13], (T5_BUCKETS, T5_HEADS), 0.5),
        "w_br_a": nrm(ks[14], (DEPTH, A_V, D), A_V ** -0.5),
        "w_br_b": nrm(ks[15], (DEPTH, B_W, D), B_W ** -0.5),
        "w_br_c": nrm(ks[16], (DEPTH, C_W, D), C_W ** -0.5),
        "w_o": nrm(ks[17], (DEPTH, D, D), D ** -0.5),
        "g_ff2": gain(ks[18], (DEPTH, D)),
        "w1_ff2": nrm(ks[19], (DEPTH, D, D_FF), D ** -0.5),
        "w3_ff2": nrm(ks[20], (DEPTH, D, D_FF), D ** -0.5),
        "w2_ff2": nrm(ks[21], (DEPTH, D_FF, D), D_FF ** -0.5),
        "g_final": gain(ks[22], (D,)),
    }

def reference(x, g_ff1, w1_ff1, w3_ff1, w2_ff1, g_mix, w_in, lam_q1, lam_k1, lam_q2, lam_k2,
              subln_g, na_rpb, t5_table, w_br_a, w_br_b, w_br_c, w_o, g_ff2, w1_ff2, w3_ff2,
              w2_ff2, g_final):
    B, S, D = x.shape
    split_idx = [int(c) for c in np.cumsum(IN_SPLITS)]
    t5_a = t5_table[:, :A_HEADS]
    t5_c = t5_table[:, A_HEADS:]
    for l in range(DEPTH):
        x = x + 0.5 * swiglu(rmsnorm(x, g_ff1[l]), w1_ff1[l], w3_ff1[l], w2_ff1[l])
        h = rmsnorm(x, g_mix[l])
        p = h @ w_in[l]
        aq, ak, av, bq, bk, bv, cq, ck, cv, gates = jnp.split(p, split_idx, axis=-1)
        lam_init = 0.8 - 0.6 * math.exp(-0.3 * l)
        lam_full = (jnp.exp(jnp.sum(lam_q1[l] * lam_k1[l])) - jnp.exp(jnp.sum(lam_q2[l] * lam_k2[l]))
                    + lam_init)
        o_a = diff_attention(aq.reshape(B, S, A_HEADS, 2, HEAD_DIM),
                             ak.reshape(B, S, A_HEADS, 2, HEAD_DIM),
                             av.reshape(B, S, A_HEADS, 2 * HEAD_DIM),
                             t5_a, lam_full, subln_g[l], lam_init)
        hd = lambda t, nh: t.reshape(B, S, nh, HEAD_DIM)
        o_b = neighborhood_attention(hd(bq, B_HEADS), hd(bk, B_HEADS), hd(bv, B_HEADS), na_rpb[l])
        o_c = dilated_attention(hd(cq, C_HEADS), hd(ck, C_HEADS), hd(cv, C_HEADS), t5_c)
        g = jax.nn.sigmoid(gates.reshape(B, S, N_BRANCH, D))
        merged = (g[:, :, 0] * (o_a @ w_br_a[l]) + g[:, :, 1] * (o_b @ w_br_b[l])
                  + g[:, :, 2] * (o_c @ w_br_c[l]))
        x = x + merged @ w_o[l]
        x = x + 0.5 * swiglu(rmsnorm(x, g_ff2[l]), w1_ff2[l], w3_ff2[l], w2_ff2[l])
    return rmsnorm(x, g_final)


_drawn_inputs = setup_inputs


def setup_inputs(seed=0):
    import zlib

    import numpy as np

    out = dict(_drawn_inputs(seed))
    spreads = {}
    factors = {'lam_q2': 5.341}
    for name, (base, spread) in spreads.items():
        noise = np.random.default_rng([zlib.crc32(name.encode()), seed]).standard_normal(out[name].shape)
        drawn = base * np.exp(spread * noise) if base else spread * noise
        out[name] = __import__('jax').numpy.asarray(drawn.astype(out[name].dtype))
    for name, factor in factors.items():
        out[name] = (out[name] * factor).astype(out[name].dtype)
    return out
```

```python
from contextlib import ExitStack
import math

import concourse.bass as bass
from concourse import mybir

F32 = mybir.dt.float32
F32R = mybir.dt.float32r
BF16 = mybir.dt.bfloat16
ALU = mybir.AluOpType
ACT = mybir.ActivationFunctionType

P = 128
D = 1024
S = 256
DEPTH = 2
DFF = 2816
TILES = S // P
KC = D // P
FC = 256
CHUNKS = DFF // FC
DH = 64
HEADS_W = 512
BLK = HEADS_W // P
A_HEADS, B_HEADS, C_HEADS = 4, 8, 8
GRID_W, NA_COLS, NA_ROWS = 64, 16, 8
EPS = 1e-6
BIG = 1e30
BC, BB, BA = 0, 1, 2
UCOLS = 2048
SLOTS = 3
CREDIT = 3

U_FFN1 = 0
U_QKV = 3 * CHUNKS
U_MIX = U_QKV + 18
MIX = ([("gate", BC, n, a) for n in range(2) for a in range(2)] + [("gate", BB, n, a) for n in range(2) for a in range(2)]
       + [("br", BC, n, 0) for n in range(2)] + [("gate", BA, n, a) for n in range(2) for a in range(2)]
       + [("br", BB, n, 0) for n in range(2)] + [("br", BA, n, 0) for n in range(2)])
U_WO = U_MIX + len(MIX)
U_FFN2 = U_WO + 4
UNITS = U_FFN2 + 3 * CHUNKS
PER_SLOT = [len(range(s, UNITS, SLOTS)) for s in range(SLOTS)]
PAIRS = 12
OT_AT = {6: [(BC, 0)], 7: [(BC, 1)], 10: [(BB, 0)], 11: [(BB, 1)], 15: [(BA, 0), (BA, 1)]}
G_FF1, G_MIX, G_FF2, SUBLN, NEGLAM, NPAR = 0, 8, 16, 24, 25, 26
T5_HEADS = A_HEADS + C_HEADS
RPB_ROWS, RPB_PITCH = 2 * NA_ROWS - 1, 128


def lam_init(l):
    return 0.8 - 0.6 * math.exp(-0.3 * l)


def bcast(ap, n):
    return bass.AP(ap.tensor, ap.offset, [list(ap.ap[0]), list(ap.ap[-1]), [0, n]])


def build(nc, x_in, stream, params_in, lam_in, g_final, t5_table, rpb, c_ident, c_mask, c_onehot, c_lncount, out):
    with ExitStack() as ctx:
        def sb(name, shape, dt=F32):
            return ctx.enter_context(nc.sbuf_tensor(name, shape, dt))

        def sem(name):
            return ctx.enter_context(nc.semaphore(name))

        raw = sb("raw", [P, SLOTS, UCOLS])
        whi = sb("whi", [P, SLOTS, UCOLS], F32R)
        wlo = sb("wlo", [P, SLOTS, UCOLS], F32R)
        x = sb("x", [P, TILES, D])
        xTh = sb("xTh", [P, KC, S], F32R)
        xTl = sb("xTl", [P, KC, S], F32R)
        nat = sb("nat", [P, 4, 512])
        silu = sb("silu", [P, TILES, FC])
        h = sb("h", [P, TILES, FC])
        hTh = sb("hTh", [P, 2, S], F32R)
        hTl = sb("hTl", [P, 2, S], F32R)
        qkT = sb("qkT", [P, 3, 2, BLK, S])
        merged = qkT[:, BC, :, :, :].rearrange("p a b s -> p a (b s)")
        v = sb("v", [P, 3, TILES, HEADS_W])
        gate = sb("gate", [P, 2, TILES, D])
        bias = sb("bias", [P, 2, 2, TILES, S])
        sneg = sb("sneg", [P, 2, TILES, S])
        probs = sb("probs", [P, 2, TILES, S])
        pT = sb("pT", [P, 2, TILES, S])
        o = sb("o", [P, 2, TILES, HEADS_W])
        oTh = sb("oTh", [P, BLK, S], F32R)
        oTl = sb("oTl", [P, BLK, S], F32R)
        ident = sb("ident", [P, P])
        ident_b = sb("ident_b", [P, P], BF16)
        mask_b = sb("mask_b", [P, S], BF16)
        params = sb("params", [P, DEPTH, NPAR])
        lay = sb("lay", [P, NPAR])
        t5_sb = sb("t5_sb", [32, T5_HEADS])
        sumsq = sb("sumsq", [P, TILES])
        meansq = sb("meansq", [P, TILES])
        rstd = sb("rstd", [P, 3, TILES])
        negmax = sb("negmax", [P, 2, TILES])
        den = sb("den", [P, 2, TILES])
        rden = [sb(f"rden{i}", [P, 2, TILES]) for i in range(4)]
        lrden = sb("lrden", [P, TILES])
        factors = sb("factors", [P, 2, TILES])
        a_sumsq = sb("a_sumsq", [P, TILES, A_HEADS])
        a_meansq = sb("a_meansq", [P, TILES * A_HEADS])
        a_rstd = sb("a_rstd", [P, TILES * A_HEADS])
        junk = sb("junk", [P, TILES, P])
        tick = sb("tick", [P, 2])
        minus_half = sb("minus_half", [P, 8])
        lam_dot = sb("lam_dot", [P, DEPTH, 2])
        lam_exp = sb("lam_exp", [P, DEPTH, 2])
        bank = [ctx.enter_context(nc.psum_tensor(f"bank{i}", [P, 512], F32)) for i in range(8)]
        t5_rows = nc.dram_tensor("t5_rows", [T5_HEADS, 512], F32, kind="Internal").ap()

        raw_landed = [sem(f"raw_landed{s}") for s in range(SLOTS)]
        x_landed, const_landed, lam_landed, t5_stored, gfin_landed, out_stored = map(
            sem, ("x_landed", "const_landed", "lam_landed", "t5_stored", "gfin_landed", "out_stored"))
        bias_landed = [sem(f"bias_landed{i}") for i in range(2)]
        half_done, unit_used, quarter_turned, h_turned, qk_turned, scores_ready, probs_turned, pv_done, o_turned, t5_product = map(
            sem, ("half_done", "unit_used", "quarter_turned", "h_turned", "qk_turned", "scores_ready", "probs_turned",
                  "pv_done", "o_turned", "t5_product"))
        hi_ready, quarter_hi, squared, silu_done, h_hi, qkv_out, gate_ready, exp_done, pT0_ready, o_hi, lam_exped = map(
            sem, ("hi_ready", "quarter_hi", "squared", "silu_done", "h_hi", "qkv_out", "gate_ready", "exp_done",
                  "pT0_ready", "o_hi", "lam_exped"))
        (unit_split, quarter_ready, quarter_scaled, quarter_split, meansq_ready, lay_ready, gated, h_split, qk_ready, biased,
         rden_ready, mixed, pT1_ready, o_ready, a_squared, a_mean, a_normed, o_split, branch_read, setup_done, lam_dotted,
         t5_biased, out_ready, a_premix, branch_added) = map(
            sem, ("unit_split", "quarter_ready", "quarter_scaled", "quarter_split", "meansq_ready", "lay_ready", "gated",
                  "h_split", "qk_ready", "biased", "rden_ready", "mixed", "pT1_ready", "o_ready", "a_squared", "a_mean",
                  "a_normed", "o_split", "branch_read", "setup_done", "lam_dotted", "t5_biased", "out_ready", "a_premix", "branch_added"))
        pool_pow, rstd_ready, a_rstd_ready, half_set = map(sem, ("pool_pow", "rstd_ready", "a_rstd_ready", "half_set"))

        def n_unit(l, u, i=0):
            return l * UNITS + (u + 1) + i * SLOTS

        def n_quarter(l, inst, q):
            return l * 16 + (4 * inst + q + 1)

        def n_scaled(l, inst, q):
            return l * 12 + (4 * (inst - (inst > 2)) + q + 1)

        def n_norm(l, j):
            return l * 3 + (j + 1)

        def n_chunk(l, f, c):
            return l * (2 * CHUNKS) + c + (f * CHUNKS + 1)

        def n_gated(l, f, c, t):
            return l * (4 * CHUNKS) + c * 2 + (2 * f * CHUNKS + t + 1)

        def n_probs_turned(l, s, m):
            return l * 20 + ((2 * s + m if s < 8 else 16 + s - 8) + 1)

        def n_branch(l, b, n, t):
            return l * 12 + (4 * b + 2 * n + t + 1)

        def n_bias(l, s):
            per = {BC: 2, BB: 8, BA: 1}
            return l * (16 * sum(per[q // 4] for q in range(s % 2, PAIRS, 2))) + 16 * sum(per[q // 4] for q in range(s % 2, s + 1, 2))

        block = ctx.enter_context(nc.Block())

        @block.sync
        def _(sp):
            def load(l, u, i):
                if u == 0:
                    sp.wait_ge(unit_split, l * UNITS + CREDIT)
                sp.wait_ge(unit_split, n_unit(l, u, i) - SLOTS + CREDIT)
                sp.dma_start(raw[:, u % SLOTS, :], stream[l * UNITS + i * SLOTS + u, :, :]).then_inc(raw_landed[u % SLOTS], 16)

            with sp.Fori(0, DEPTH) as l:
                with sp.Fori(0, UNITS // SLOTS) as i:
                    for u in range(SLOTS):
                        load(l, u, i)
                load(l, UNITS - 1, 0)
            sp.wait_ge(out_ready, 1)
            sp.dma_start(out[0, 0:P, :], nat[:, 0:2, :].rearrange("p a b -> p (a b)")).then_inc(out_stored, 16)
            sp.wait_ge(out_ready, 2)
            sp.dma_start(out[0, P:S, :], nat[:, 2:4, :].rearrange("p a b -> p (a b)")).then_inc(out_stored, 16)
            sp.wait_ge(out_stored, 32)

        @block.gpsimd
        def _(pool):
            pool.memset(minus_half[:, :], -0.5).then_inc(half_set, 1)
            pool.memset(factors[:, 0, :], 0.5).then_inc(half_set, 1)
            pool.memset(factors[:, 1, :], 0.125).then_inc(half_set, 1)
            pool.wait_ge(half_set, 3)

            def inverse_rms(l, j):
                pool.wait_ge(meansq_ready, n_norm(l, j))
                pool.tensor_tensor(rstd[:, 0, :], meansq[:, :], minus_half[:, 0:TILES], ALU.pow).then_inc(pool_pow, 1)
                pool.wait_ge(pool_pow, n_norm(l, j))
                one = rstd[:, 0, :]
                both = bass.AP(one.tensor, one.offset, [list(one.ap[0]), [0, 2], [1, TILES]])
                pool.tensor_tensor(rstd[:, 1:3, :], both, factors[:, :, :], ALU.mult).then_inc(rstd_ready, 1)

            with pool.Fori(0, DEPTH) as l:
                inverse_rms(l, 0)
                inverse_rms(l, 1)
                pool.wait_ge(a_mean, l + 1)
                pool.tensor_tensor(a_rstd[:, :], a_meansq[:, :], minus_half[:, :], ALU.pow).then_inc(a_rstd_ready, 1)
                inverse_rms(l, 2)
            inverse_rms(DEPTH, 0)

        @block.scalar
        def _(act):
            act.dma_start(ident[:, :], c_ident).then_inc(const_landed, 16)
            act.dma_start(x[:, :, :], x_in[0].rearrange("(t p) d -> p t d", p=P)).then_inc(x_landed, 16)
            act.dma_start(probs[:, 0, 0, :], c_mask).then_inc(const_landed, 16)
            act.dma_start(sneg[0:32, 0, :, :].rearrange("p a b -> p (a b)"), c_onehot).then_inc(const_landed, 16)
            act.dma_start(pT[0:T5_HEADS, 0, :, :].rearrange("p a b -> p (a b)"), c_lncount).then_inc(const_landed, 16)
            act.dma_start(t5_sb[:, :], t5_table).then_inc(const_landed, 16)
            act.dma_start(params[:, :, 0:NEGLAM], params_in).then_inc(const_landed, 16)
            act.dma_start(nat[:, 0, :], bass.AP(lam_in.tensor, 0, [[0, P], [1, DEPTH * 4 * DH]])).then_inc(lam_landed, 16)

            act.wait_ge(lam_dotted, 4)
            act.activation(lam_exp[:, :, :], lam_dot[:, :, :], ACT.Exp).then_inc(lam_exped, 1)
            act.wait_ge(t5_biased, 1)
            act.dma_start(t5_rows, pT[0:T5_HEADS, 1, :, :].rearrange("p a b -> p (a b)")).then_inc(t5_stored, 16)

            def to_hi(l, u, i=0):
                if u >= UNITS:
                    return
                s = u % SLOTS
                if u < SLOTS:
                    act.wait_ge(unit_used, l * UNITS + CREDIT)
                else:
                    act.wait_ge(unit_used, n_unit(l, u - SLOTS, i) + CREDIT)
                act.wait_ge(raw_landed[s], (l * PER_SLOT[s] + i + (u // SLOTS + 1)) * 16)
                act.activation(whi[:, s, :], raw[:, s, :], ACT.Copy).then_inc(hi_ready, 1)

            def quarter(l, inst, q):
                t, n = q % 2, q // 2
                dst = xTh[:, 4 * n:4 * n + 4, t * P:(t + 1) * P]
                if inst == 2:
                    act.wait_ge(quarter_turned, n_quarter(l, inst, q))
                    src = bank[6 + q % 2][:, :]
                else:
                    act.wait_ge(quarter_scaled, n_scaled(l, inst, q))
                    src = nat[:, q, :]
                act.activation(dst, src.rearrange("p (a b) -> p a b", a=4), ACT.Copy).then_inc(quarter_hi, 1)

            def squares(l, inst):
                for t in range(TILES):
                    act.wait_ge(quarter_ready, n_quarter(l, inst, 2 + t))
                    act.activation((probs, sneg)[t][:, :, :, :].rearrange("p a b c -> p (a b c)"), x[:, t, :], ACT.Square,
                                   accum_out=sumsq[:, t:t + 1]).then_inc(squared, 1)

            def h_to_hi(l, f, c):
                act.wait_ge(h_turned, n_chunk(l, f, c))
                act.activation(hTh[:, :, :], bank[6][:, :].rearrange("p (a b) -> p a b", a=2), ACT.Copy).then_inc(h_hi, 1)

            def gates_silu(l, f, c, u, i=0):
                for t in range(TILES):
                    if t == 0:
                        act.wait_ge(half_done, n_unit(l, u, i))
                    else:
                        act.wait_ge(unit_used, n_unit(l, u, i) + CREDIT)
                    act.activation(silu[:, t, :], bank[4 + t][:, 0:FC], ACT.Silu, scale=rstd[:, 0, t:t + 1]).then_inc(silu_done, 1)

            def ffn(l, f, u0, j):
                to_hi(l, u0 + 3)
                act.wait_ge(rstd_ready, n_norm(l, j))
                gates_silu(l, f, 0, u0 + 1)
                to_hi(l, u0 + 4)

                def chunk(c, u, i):
                    h_to_hi(l, f, c - 1)
                    to_hi(l, u + 3, i)
                    gates_silu(l, f, c, u + 1, i)
                    to_hi(l, u + 4, i)
                    to_hi(l, u + 5, i)

                chunk(1, u0 + 2, 0)
                with act.Fori(0, CHUNKS - 3) as i:
                    chunk(i + 2, u0 + 5, i)
                chunk(CHUNKS - 1, u0 + 3 * CHUNKS - 4, 0)
                h_to_hi(l, f, CHUNKS - 1)

            def load_bias(l, s):
                b, blk, ring = s // 4, s % 4, s % 2
                if b == BB:
                    for m in range(2):
                        for half in range(2):
                            for t in range(TILES):
                                row = (2 * blk + m) * RPB_ROWS + NA_ROWS - 4 + half + 2 * t
                                src = bass.AP(rpb.tensor, row * RPB_PITCH, [[B_HEADS * RPB_ROWS * RPB_PITCH, DEPTH], [1, GRID_W],
                                                                            [RPB_PITCH, 4], [1, GRID_W]])
                                act.dma_start(bias[64 * half:64 * half + 64, ring, m, t, :].rearrange("p (r c) -> p r c", r=4),
                                              src[l]).then_inc(bias_landed[ring], 16)
                    return
                for m in range(1 if b == BA else 2):
                    head = blk if b == BA else A_HEADS + 2 * blk + m
                    src = bass.AP(t5_rows.tensor, head * 512, [[1, P], [P, TILES], [1, S]])
                    act.dma_start(bias[:, ring, m, :, :], src).then_inc(bias_landed[ring], 16)

            act.wait_ge(t5_stored, 16)
            with act.Fori(0, DEPTH) as l:
                to_hi(l, 0)
                quarter(l, 0, 0)
                quarter(l, 0, 1)
                to_hi(l, 1)
                squares(l, 0)
                quarter(l, 0, 2)
                quarter(l, 0, 3)
                to_hi(l, 2)
                ffn(l, 0, U_FFN1, 0)
                load_bias(l, 0)
                load_bias(l, 1)
                quarter(l, 1, 0)
                quarter(l, 1, 1)
                squares(l, 1)
                quarter(l, 1, 2)
                quarter(l, 1, 3)
                to_hi(l, U_QKV + 2)
                act.wait_ge(rstd_ready, n_norm(l, 1))
                with act.Fori(0, 3) as b:
                    for c in range(3):
                        u = U_QKV + 2 * c
                        to_hi(l, u + 3, b * 2)
                        for t in range(TILES):
                            if t == 0:
                                act.wait_ge(half_done, n_unit(l, u + 1, b * 2))
                            else:
                                act.wait_ge(unit_used, n_unit(l, u + 1, b * 2) + CREDIT)
                            dst = v[:, b, t, :] if c == 2 else nat[:, 2 * c + t, :]
                            scale = rstd[:, 2, t:t + 1] if c == 0 else rstd[:, 0, t:t + 1]
                            act.activation(dst, bank[2 * c + t][:, :], ACT.Copy, scale=scale).then_inc(qkv_out, 1)
                        to_hi(l, u + 4, b * 2)
                for j in range(len(MIX) + 4):
                    u = U_MIX + j
                    kind, b, n, a = MIX[j] if j < len(MIX) else ("wo", 0, 0, 0)
                    if kind == "gate" and a == 1:
                        for t in range(TILES):
                            if t == 0:
                                act.wait_ge(half_done, n_unit(l, u))
                            else:
                                act.wait_ge(unit_used, n_unit(l, u) + CREDIT)
                            act.activation(gate[:, b % 2, t, n * 512:(n + 1) * 512], bank[t][:, :], ACT.Tanh,
                                           scale=rstd[:, 1, t:t + 1]).then_inc(gate_ready, 1)
                    if 1 <= j <= PAIRS:
                        act.wait_ge(probs_turned, n_probs_turned(l, j - 1, 0))
                        act.activation(pT[:, 0, :, :], bank[4][:, :].rearrange("p (a b) -> p a b", a=2),
                                       ACT.Copy).then_inc(pT0_ready, 1)
                    if j < PAIRS:
                        if j >= 1:
                            act.wait_ge(probs_turned, n_probs_turned(l, j - 1, 0 if j - 1 >= 8 else 1))
                        for m in range(2):
                            act.wait_ge(biased, l * 24 + 2 * j + m + 1)
                            for t in range(TILES):
                                e = act.activation(probs[:, m, t, ::-1], sneg[:, m, t, :], ACT.Exp, scale=-1.0,
                                                   bias=negmax[:, m, t:t + 1], accum_out=den[:, m, t:t + 1])
                            e.then_inc(exp_done, 1)
                    if j < PAIRS - 2:
                        load_bias(l, j + 2)
                    for b2, half in OT_AT.get(j, []):
                        act.wait_ge(o_turned, l * 6 + 2 * b2 + half + 1)
                        act.activation(oTh[:, 2 * half:2 * half + 2, :], bank[7][:, :].rearrange("p (a b) -> p a b", a=2), ACT.Copy,
                                       **({"scale": lay[:, SUBLN:SUBLN + 1]} if b2 == BA else {})).then_inc(o_hi, 1)
                    if kind == "wo" and j == len(MIX):
                        quarter(l, 2, 2)
                        quarter(l, 2, 3)
                    if j < len(MIX) + 3:
                        to_hi(l, u + 3)
                    if j == len(MIX) - 1:
                        quarter(l, 2, 0)
                        quarter(l, 2, 1)
                quarter(l, 3, 0)
                quarter(l, 3, 1)
                squares(l, 3)
                quarter(l, 3, 2)
                quarter(l, 3, 3)
                to_hi(l, U_FFN2 + 2)
                ffn(l, 1, U_FFN2, 2)
            act.dma_start(gate[:, 0, 0, :], bass.AP(g_final.tensor, 0, [[0, P], [1, D]])).then_inc(gfin_landed, 16)
            squares(DEPTH, 0)

        @block.tensor
        def _(pe):
            def three(dst, sh, sl, mh, ml, start, stop):
                pe.matmul(dst, sh, mh, start=start, stop=False)
                pe.matmul(dst, sh, ml, start=False, stop=False)
                return pe.matmul(dst, sl, mh, start=False, stop=stop)

            def unit_rows(l, u, i, th, tl, k0, dst, start, stop, before=(None, None), mid=None):
                s = u % SLOTS
                pe.wait_ge(unit_split, n_unit(l, u, i) + CREDIT)
                for t in range(TILES):
                    if t == 1 and mid:
                        mid()
                    if before[t]:
                        before[t]()
                    for k in range(4):
                        cols, w = slice(t * P, (t + 1) * P), slice(k * 512, (k + 1) * 512)
                        last = three(dst[t], th[:, k0 + k, cols], tl[:, k0 + k, cols], whi[:, s, w], wlo[:, s, w],
                                     start and k == 0, stop and k == 3)
                    last.then_inc(half_done if t == 0 else unit_used, 1)

            def turn_quarter(l, inst, q):
                t, n = q % 2, q // 2
                src = merged if inst == 2 else x
                pe.wait_ge(quarter_ready, n_quarter(l, inst, q))
                if q >= 2:
                    if inst == 2:
                        pe.wait_ge(quarter_split, n_quarter(l, inst, q - 2))
                    else:
                        pe.wait_ge(quarter_scaled, n_scaled(l, inst, q - 2))
                for k in range(4):
                    c = (4 * n + k) * P
                    last = pe.transpose(bank[6 + q % 2][:, k * P:(k + 1) * P], src[:, t, c:c + P], ident[:, :])
                last.then_inc(quarter_turned, 1)

            def split(l, inst, q):
                return lambda: pe.wait_ge(quarter_split, n_quarter(l, inst, q))

            def later_quarters(l, inst):
                def go():
                    turn_quarter(l, inst, 2)
                    turn_quarter(l, inst, 3)
                return go

            def ffn(l, f, u0, inst):
                ab = [bank[4][:, :], bank[5][:, :]]

                def up(c, u, i, a):
                    free = (lambda: pe.wait_ge(gated, n_gated(l, f, c - 1, 0)), lambda: pe.wait_ge(gated, n_gated(l, f, c - 1, 1)))
                    unit_rows(l, u, i, xTh, xTl, 4 * a, ab, a == 0, a == 1, before=free if a == 0 else (None, None))

                def turn_h(c):
                    pe.wait_ge(gated, n_gated(l, f, c, 1))
                    for t in range(TILES):
                        for j in range(2):
                            last = pe.transpose(bank[6][:, j * S + t * P:j * S + (t + 1) * P], h[:, t, j * P:(j + 1) * P], ident[:, :])
                    last.then_inc(h_turned, 1)

                def down(c, u, i, start, stop):
                    s = u % SLOTS
                    pe.wait_ge(unit_split, n_unit(l, u, i) + CREDIT)
                    pe.wait_ge(h_split, n_chunk(l, f, c))
                    for n in range(2):
                        for t in range(TILES):
                            for j in range(2):
                                cols, w = slice(t * P, (t + 1) * P), slice(j * D + n * 512, j * D + (n + 1) * 512)
                                last = three(bank[2 * n + t][:, :], hTh[:, j, cols], hTl[:, j, cols], whi[:, s, w], wlo[:, s, w],
                                             start and j == 0, stop and j == 1)
                        last.then_inc(half_done if n == 0 else unit_used, 1)

                turn_quarter(l, inst, 0)
                turn_quarter(l, inst, 1)
                unit_rows(l, u0, 0, xTh, xTl, 0, ab, True, False, before=(split(l, inst, 0), split(l, inst, 1)), mid=later_quarters(l, inst))
                unit_rows(l, u0 + 1, 0, xTh, xTl, 4, ab, False, True, before=(split(l, inst, 2), split(l, inst, 3)))

                def chunk(c, u, i, start=False):
                    up(c, u, i, 0)
                    turn_h(c - 1)
                    up(c, u + 1, i, 1)
                    down(c - 1, u + 2, i, start, False)

                chunk(1, u0 + 2, 0, start=True)
                with pe.Fori(0, CHUNKS - 3) as i:
                    chunk(i + 2, u0 + 5, i)
                chunk(CHUNKS - 1, u0 + 3 * CHUNKS - 4, 0)
                turn_h(CHUNKS - 1)
                down(CHUNKS - 1, u0 + 3 * CHUNKS - 1, 0, False, True)

            pe.sem_inc(unit_used, CREDIT)
            pe.wait_ge(const_landed, 96)
            pe.matmul(bank[7][0:T5_HEADS, :], t5_sb[:, :], sneg[0:32, 0, :, :], start=True, stop=True).then_inc(t5_product, 1)

            with pe.Fori(0, DEPTH) as l:
                ffn(l, 0, U_FFN1, 0)
                turn_quarter(l, 1, 0)
                turn_quarter(l, 1, 1)
                u = U_QKV

                def turn_qk(b, c):
                    pe.wait_ge(qkv_out, l * 18 + b * 6 + (2 * c + 2))
                    for m in range(2):
                        pe.wait_ge(qk_ready, l * 12 + b * 4 + (2 * c + m + 1 - 2 + 4))
                        for blk in (2 * m, 2 * m + 1):
                            for t in range(TILES):
                                last = pe.transpose(bank[6 + m][:, (blk % 2) * S + t * P:(blk % 2) * S + (t + 1) * P],
                                                    nat[:, 2 * c + t, blk * P:(blk + 1) * P], ident[:, :])
                        last.then_inc(qk_turned, 1)

                later_quarters(l, 1)()
                with pe.Fori(0, 3) as b:
                    pe.wait_ge(quarter_split, n_quarter(l, 1, 3))
                    for c in range(3):
                        dst = [bank[2 * c][:, :], bank[2 * c + 1][:, :]]
                        unit_rows(l, u + 2 * c, b * 2, xTh, xTl, 0, dst, True, False)
                        if c:
                            turn_qk(b, c - 1)
                        unit_rows(l, u + 2 * c + 1, b * 2, xTh, xTl, 4, dst, False, True)
                pr = [bank[0][:, :], bank[1][:, :]]

                def scores(s):
                    b, blk = s // 4, s % 4
                    if s == 0:
                        pe.wait_ge(qk_ready, l * 12 + 12 + 4)
                    for m in range(2):
                        if s:
                            pe.wait_ge(biased, l * 24 + 2 * (s - 1) + m + 1)
                        rows = slice(DH * m, DH * m + DH)
                        for t in range(TILES):
                            dst = bank[2 + m][:, t * S:(t + 1) * S]
                            last = pe.matmul(dst, qkT[rows, b, 0, blk, t * P:(t + 1) * P], qkT[rows, b, 1, blk, :],
                                             start=True, stop=b != BB)
                            if b == BB:
                                last = pe.matmul(dst, ident_b[:, :], mask_b[:, :], start=False, stop=True)
                        last.then_inc(scores_ready, 1)

                def turn_probs(s):
                    b = s // 4
                    if s == 0:
                        pe.wait_ge(qkv_out, l * 18 + 18)
                    else:
                        pe.wait_ge(pT0_ready, l * 12 + s)
                        if s <= 8:
                            pe.wait_ge(pT1_ready, l * 8 + s)
                    for m in range(1 if b == BA else 2):
                        if b == BA:
                            pe.wait_ge(mixed, l * 4 + (s - 8) + 1)
                        else:
                            pe.wait_ge(exp_done, l * 24 + 2 * s + m + 1)
                        for kb in range(TILES):
                            for t in range(TILES):
                                last = pe.transpose(bank[4 + m][:, kb * S + t * P:kb * S + (t + 1) * P],
                                                    probs[:, m, t, kb * P:(kb + 1) * P], ident[:, :])
                        last.then_inc(probs_turned, 1)

                def values(s):
                    b, blk = s // 4, s % 4
                    pe.wait_ge(pT0_ready, l * 12 + s + 1)
                    if b != BA:
                        pe.wait_ge(pT1_ready, l * 8 + s + 1)
                    if s:
                        pe.wait_ge(o_ready, l * 12 + s)
                    maps, w = (1, P) if b == BA else (2, DH)
                    for t in range(TILES):
                        for m in range(maps):
                            c = blk * P + m * DH
                            for kb in range(TILES):
                                last = pe.matmul(bank[6][:, t * P + m * DH:t * P + m * DH + w], pT[:, m, kb, t * P:(t + 1) * P],
                                                 v[:, b, kb, c:c + w], start=kb == 0, stop=kb == 1)
                    last.then_inc(pv_done, 1)

                def turn_o(b, half):
                    if half == 0:
                        if b == BA:
                            pe.wait_ge(a_normed, l + 1)
                        else:
                            pe.wait_ge(o_ready, l * 12 + 4 * b + 4)
                    if 2 * b + half:
                        pe.wait_ge(o_split, l * 6 + 2 * b + half)
                    for k in range(2):
                        blk = 2 * half + k
                        for t in range(TILES):
                            last = pe.transpose(bank[7][:, k * S + t * P:k * S + (t + 1) * P], o[:, b % 2, t, blk * P:(blk + 1) * P],
                                                ident[:, :])
                    last.then_inc(o_turned, 1)

                def products_read(j):
                    kind, b, n, _ = MIX[j - 1]
                    ready = gate_ready if kind == "gate" else branch_read
                    return tuple((lambda t=t: pe.wait_ge(ready, n_branch(l, b, n, t))) for t in range(TILES))

                for j, (kind, b, n, a) in enumerate(MIX):
                    before = products_read(j) if j and a == 0 else (None, None)
                    if kind == "gate":
                        unit_rows(l, U_MIX + j, 0, xTh, xTl, 4 * a, pr, a == 0, a == 1, before=before)
                    else:
                        if n == 0:
                            pe.wait_ge(o_split, l * 6 + 2 * b + 2)
                        unit_rows(l, U_MIX + j, 0, oTh, oTl, 0, pr, True, True, before=before)
                    if j < PAIRS:
                        scores(j)
                    if 2 <= j < PAIRS + 2:
                        values(j - 2)
                    if 1 <= j <= PAIRS:
                        turn_probs(j - 1)
                    for b2, half in OT_AT.get(j, []):
                        turn_o(b2, half)
                turn_quarter(l, 2, 0)
                turn_quarter(l, 2, 1)
                for n in range(2):
                    for a in range(2):
                        unit_rows(l, U_WO + 2 * n + a, 0, xTh, xTl, 4 * a, [bank[2 * n][:, :], bank[2 * n + 1][:, :]], a == 0, a == 1,
                                  before=(split(l, 2, 2 * a), split(l, 2, 2 * a + 1)) if n == 0 else (None, None),
                                  mid=later_quarters(l, 2) if n == a == 0 else None)
                ffn(l, 1, U_FFN2, 3)

        @block.vector
        def _(dve):
            dve.sem_inc(unit_split, CREDIT)
            dve.sem_inc(qk_ready, 4)
            dve.wait_ge(const_landed, 96)
            dve.tensor_copy(ident_b[:, :], ident[:, :]).then_inc(setup_done, 1)
            dve.tensor_copy(mask_b[:, :], probs[:, 0, 0, :]).then_inc(setup_done, 1)
            dve.wait_ge(lam_landed, 16)
            for l in range(DEPTH):
                for k in range(2):
                    at = (l * 4 + 2 * k) * DH
                    dve.tensor_tensor_reduce(out=nat[:, 1, at:at + DH], in0=nat[:, 0, at:at + DH], in1=nat[:, 0, at + DH:at + 2 * DH],
                                             scale=1.0, scalar=0.0, op0=ALU.mult, op1=ALU.add,
                                             accum_out=lam_dot[:, l, k:k + 1]).then_inc(lam_dotted, 1)
            dve.wait_ge(lam_exped, 1)
            for l in range(DEPTH):
                dve.scalar_tensor_tensor(out=params[:, l, NEGLAM:NEGLAM + 1], in0=lam_exp[:, l, 1:2], scalar=-lam_init(l),
                                         in1=lam_exp[:, l, 0:1], op0=ALU.add, op1=ALU.subtract).then_inc(setup_done, 1)
                dve.tensor_scalar(params[:, l, SUBLN:SUBLN + 1], params[:, l, SUBLN:SUBLN + 1], 1.0 - lam_init(l), None,
                                  ALU.mult).then_inc(setup_done, 1)
            dve.wait_ge(t5_product, 1)
            dve.tensor_tensor(pT[0:T5_HEADS, 1, :, :].rearrange("p a b -> p (a b)"), bank[7][0:T5_HEADS, :],
                              pT[0:T5_HEADS, 0, :, :].rearrange("p a b -> p (a b)"), ALU.add).then_inc(t5_biased, 1)
            dve.wait_ge(setup_done, 6)
            dve.wait_ge(t5_biased, 1)
            dve.wait_ge(x_landed, 16)
            dve.sem_inc(quarter_ready, 4)

            def to_lo(l, u, i=0):
                if u >= UNITS:
                    return
                s = u % SLOTS
                dve.wait_ge(hi_ready, n_unit(l, u, i))
                dve.tensor_tensor(wlo[:, s, :], raw[:, s, :], whi[:, s, :].bitcast(F32), ALU.subtract).then_inc(unit_split, 1)

            def scale_quarter(l, inst, q):
                g = {0: G_FF1, 1: G_MIX, 3: G_FF2}[inst] + 4 * (q // 2)
                dve.wait_ge(quarter_turned, n_quarter(l, inst, q))
                dve.tensor_tensor(nat[:, q, :].rearrange("p (a b) -> p a b", a=4),
                                  bank[6 + q % 2][:, :].rearrange("p (a b) -> p a b", a=4),
                                  bcast(lay[:, g:g + 4], P), ALU.mult).then_inc(quarter_scaled, 1)

            def split_quarter(l, inst, q):
                t, n = q % 2, q // 2
                src = bank[6 + q % 2][:, :] if inst == 2 else nat[:, q, :]
                cols = (slice(None), slice(4 * n, 4 * n + 4), slice(t * P, (t + 1) * P))
                dve.wait_ge(quarter_hi, n_quarter(l, inst, q))
                dve.tensor_tensor(xTl[cols], src.rearrange("p (a b) -> p a b", a=4), xTh[cols].bitcast(F32),
                                  ALU.subtract).then_inc(quarter_split, 1)

            def two_quarters(l, inst, q):
                for k in (q, q + 1):
                    scale_quarter(l, inst, k)
                for k in (q, q + 1):
                    split_quarter(l, inst, k)

            def mean_squares(l, j):
                dve.wait_ge(squared, n_norm(l, j) * 2)
                dve.tensor_scalar(meansq[:, :], sumsq[:, :], 1.0 / D, EPS, ALU.mult, ALU.add).then_inc(meansq_ready, 1)

            def residual(q):
                t, n = q % 2, q // 2
                w = slice(n * 512, (n + 1) * 512)
                dve.scalar_tensor_tensor(out=x[:, t, w], in0=bank[q][:, :], scalar=0.5, in1=x[:, t, w], op0=ALU.mult,
                                         op1=ALU.add).then_inc(quarter_ready, 1)

            def h_to_lo(l, f, c):
                dve.wait_ge(h_hi, n_chunk(l, f, c))
                dve.tensor_tensor(hTl[:, :, :], bank[6][:, :].rearrange("p (a b) -> p a b", a=2), hTh[:, :, :].bitcast(F32),
                                  ALU.subtract).then_inc(h_split, 1)

            def gated_h(l, f, c):
                for t in range(TILES):
                    dve.wait_ge(silu_done, n_gated(l, f, c, t))
                    dve.scalar_tensor_tensor(out=h[:, t, :], in0=bank[4 + t][:, FC:2 * FC], scalar=rstd[:, 0, t:t + 1],
                                             in1=silu[:, t, :], op0=ALU.mult, op1=ALU.mult).then_inc(gated, 1)

            def ffn(l, f, u0):
                to_lo(l, u0 + 3)
                gated_h(l, f, 0)
                to_lo(l, u0 + 4)

                def chunk(c, u, i):
                    h_to_lo(l, f, c - 1)
                    to_lo(l, u + 3, i)
                    gated_h(l, f, c)
                    to_lo(l, u + 4, i)
                    to_lo(l, u + 5, i)

                chunk(1, u0 + 2, 0)
                with dve.Fori(0, CHUNKS - 3) as i:
                    chunk(i + 2, u0 + 5, i)
                chunk(CHUNKS - 1, u0 + 3 * CHUNKS - 4, 0)
                h_to_lo(l, f, CHUNKS - 1)
                u = u0 + 3 * CHUNKS - 1
                dve.wait_ge(half_done, n_unit(l, u))
                residual(0)
                residual(1)
                dve.wait_ge(unit_used, n_unit(l, u) + CREDIT)
                residual(2)
                residual(3)

            with dve.Fori(0, DEPTH) as l:
                dve.tensor_copy(lay[:, :], params[:, l, :]).then_inc(lay_ready, 1)
                dve.wait_ge(lay_ready, l + 1)
                to_lo(l, 0)
                two_quarters(l, 0, 0)
                to_lo(l, 1)
                two_quarters(l, 0, 2)
                mean_squares(l, 0)
                to_lo(l, 2)
                ffn(l, 0, U_FFN1)
                two_quarters(l, 1, 0)
                two_quarters(l, 1, 2)
                mean_squares(l, 1)
                to_lo(l, U_QKV + 2)

                def evacuate_qk(b, c):
                    for m in range(2):
                        dve.wait_ge(qk_turned, l * 12 + b * 4 + (2 * c + m + 1))
                        src = bank[6 + m][:, :].rearrange("p (a b) -> p a b", a=2)
                        dve.tensor_copy(qkT[:, b, c, 2 * m:2 * m + 2, :], src if c == 0 else src[:, :, ::-1]).then_inc(qk_ready, 1)

                with dve.Fori(0, 3) as b:
                    for c in range(3):
                        u = U_QKV + 2 * c
                        to_lo(l, u + 3, b * 2)
                        if c:
                            evacuate_qk(b, c - 1)
                        to_lo(l, u + 4, b * 2)

                def add_branch(b, n, u):
                    w = slice(n * 512, (n + 1) * 512)
                    for t in range(TILES):
                        if t == 0:
                            dve.wait_ge(half_done, n_unit(l, u))
                        else:
                            dve.wait_ge(unit_used, n_unit(l, u) + CREDIT)
                        dve.wait_ge(gate_ready, n_branch(l, b, n, t))
                        dve.scalar_tensor_tensor(out=merged[:, t, w] if b == BC else nat[:, 2 * n + t, :],
                                                 in0=gate[:, b % 2, t, w], scalar=1.0, in1=bank[t][:, :], op0=ALU.add,
                                                 op1=ALU.mult).then_inc(branch_read, 1)
                    if b == BC:
                        return
                    for t in range(TILES):
                        dve.wait_ge(branch_read, n_branch(l, b, n, t))
                        add = dve.tensor_tensor(merged[:, t, w], merged[:, t, w], nat[:, 2 * n + t, :], ALU.add)
                        add.then_inc(quarter_ready if b == BA else branch_added, 1)

                def add_bias(s):
                    b, ring = s // 4, s % 2
                    dve.wait_ge(bias_landed[ring], n_bias(l, s))
                    if s:
                        dve.wait_ge(exp_done, l * 24 + 2 * s)
                    for m in range(2):
                        dve.wait_ge(scores_ready, l * 24 + 2 * s + m + 1)
                        dve.memset(tick[:, m:m + 1], 0.0)
                        for t in range(TILES):
                            r = dve.tensor_tensor_reduce(out=sneg[:, m, t, :], in0=bank[2 + m][:, t * S:(t + 1) * S],
                                                         in1=bias[:, ring, 0 if b == BA else m, t, :], scale=-1.0, scalar=3e38,
                                                         op0=ALU.add, op1=ALU.min, accum_out=negmax[:, m, t:t + 1])
                        r.then_inc(biased, 1)

                def read_values(s):
                    b, blk = s // 4, s % 4
                    dve.wait_ge(pv_done, l * 12 + s + 1)
                    if b == BA:
                        dst = o[:, 0, :, blk * P:(blk + 1) * P]
                        dve.tensor_copy(dst, bank[6][:, 0:2 * P].rearrange("p (a b) -> p a b", a=2)).then_inc(o_ready, 1)
                        dve.wait_ge(o_ready, l * 12 + s + 1)
                        for t in range(TILES):
                            r = dve.tensor_tensor_reduce(out=junk[:, t, :], in0=o[:, 0, t, blk * P:(blk + 1) * P],
                                                         in1=o[:, 0, t, blk * P:(blk + 1) * P], scale=1.0, scalar=0.0, op0=ALU.mult,
                                                         op1=ALU.add, accum_out=a_sumsq[:, t, blk:blk + 1])
                        r.then_inc(a_squared, 1)
                        return
                    dve.wait_ge(rden_ready, l * 12 + s + 1)
                    for m in range(2):
                        for t in range(TILES):
                            r = dve.tensor_scalar(o[:, b % 2, t, blk * P + m * DH:blk * P + (m + 1) * DH],
                                                  bank[6][:, t * P + m * DH:t * P + (m + 1) * DH], rden[s % 4][:, m, t:t + 1], None,
                                                  ALU.mult)
                    r.then_inc(o_ready, 1)

                for j in range(len(MIX) + 4):
                    u = U_MIX + j
                    kind, b, n, a = MIX[j] if j < len(MIX) else ("wo", 0, 0, 0)
                    if kind == "br":
                        add_branch(b, n, u)
                    if j < PAIRS:
                        add_bias(j)
                    if 2 <= j < PAIRS + 2:
                        read_values(j - 2)
                    if 1 <= j <= 8:
                        dve.wait_ge(probs_turned, n_probs_turned(l, j - 1, 1))
                        dve.tensor_copy(pT[:, 1, :, :], bank[5][:, :].rearrange("p (a b) -> p a b", a=2)).then_inc(pT1_ready, 1)
                    if j == PAIRS + 2:
                        dve.wait_ge(a_squared, l * 4 + 4)
                        dve.tensor_scalar(a_meansq[:, :], a_sumsq[:, :, :].rearrange("p a b -> p (a b)"), 1.0 / P, EPS, ALU.mult,
                                          ALU.add).then_inc(a_mean, 1)
                        dve.wait_ge(a_rstd_ready, l + 1)
                        oa = o[:, 0, :, :].rearrange("p t (a b) -> p (t a) b", b=P)
                        dve.tensor_tensor(oa, oa, bcast(a_rstd[:, :], P), ALU.mult).then_inc(a_normed, 1)
                    for b2, half in OT_AT.get(j, []):
                        src = bank[7][:, :].rearrange("p (a b) -> p a b", a=2)
                        w = slice(2 * half, 2 * half + 2)
                        dve.wait_ge(o_hi, l * 6 + 2 * b2 + half + 1)
                        dve.scalar_tensor_tensor(out=oTl[:, w, :], in0=src, scalar=lay[:, SUBLN:SUBLN + 1] if b2 == BA else 1.0,
                                                 in1=oTh[:, w, :].bitcast(F32), op0=ALU.mult, op1=ALU.subtract).then_inc(o_split, 1)
                    if j < PAIRS:
                        dve.wait_ge(exp_done, l * 24 + 2 * j + 2)
                        dve.reciprocal(rden[j % 4][:, :, :], den[:, :, :]).then_inc(rden_ready, 1)
                        if j >= 8:
                            r = rden[j % 4]
                            dve.wait_ge(rden_ready, l * 12 + j + 1)
                            dve.tensor_scalar(lrden[:, :], r[:, 1, :], lay[:, NEGLAM:NEGLAM + 1], None, ALU.mult)
                            for t in range(TILES):
                                w = dve.tensor_scalar(probs[:, 0, t, :], probs[:, 0, t, :], r[:, 0, t:t + 1], None, ALU.mult)
                            w.then_inc(a_premix, 1)
                            dve.wait_ge(a_premix, l * 4 + (j - 8) + 1)
                            for t in range(TILES):
                                w = dve.scalar_tensor_tensor(out=probs[:, 0, t, :], in0=probs[:, 1, t, :], scalar=lrden[:, t:t + 1],
                                                             in1=probs[:, 0, t, :], op0=ALU.mult, op1=ALU.add)
                            w.then_inc(mixed, 1)
                    if kind == "wo" and j == len(MIX):
                        split_quarter(l, 2, 2)
                        split_quarter(l, 2, 3)
                    if j < len(MIX) + 3:
                        to_lo(l, u + 3)
                    if j == len(MIX) - 1:
                        split_quarter(l, 2, 0)
                        split_quarter(l, 2, 1)
                    if j == len(MIX) + 1 or j == len(MIX) + 3:
                        q = j - len(MIX) - 1
                        dve.wait_ge(half_done, n_unit(l, u))
                        residual(q)
                        dve.wait_ge(unit_used, n_unit(l, u) + CREDIT)
                        residual(q + 1)
                two_quarters(l, 3, 0)
                two_quarters(l, 3, 2)
                mean_squares(l, 2)
                to_lo(l, U_FFN2 + 2)
                ffn(l, 1, U_FFN2)
            mean_squares(DEPTH, 0)
            dve.wait_ge(rstd_ready, n_norm(DEPTH, 0))
            dve.wait_ge(gfin_landed, 16)
            for t in range(TILES):
                dve.scalar_tensor_tensor(out=nat[:, 2 * t:2 * t + 2, :].rearrange("p a b -> p (a b)"), in0=x[:, t, :],
                                         scalar=rstd[:, 0, t:t + 1], in1=gate[:, 0, 0, :], op0=ALU.mult,
                                         op1=ALU.mult).then_inc(out_ready, 1)


def shape_constants():
    import numpy as np
    delta = 255 - np.arange(511)
    n = np.abs(delta)
    large = 8 + (np.log(np.maximum(n, 1).astype(np.float32) / 8) / math.log(1024 / 8) * 8).astype(np.int32)
    bucket = np.where(delta > 0, 16, 0) + np.where(n < 8, n, np.minimum(large, 15))
    onehot = np.zeros((32, 512), np.float32)
    onehot[bucket, np.arange(511)] = 1
    count = (n <= 64).astype(int) + (delta % 4 == 0) + (delta % 16 == 0)
    lncount = np.zeros((T5_HEADS, 512), np.float32)
    lncount[A_HEADS:, :511] = np.where(count > 0, np.log(np.maximum(count, 1)), -BIG)
    col = np.arange(P) % GRID_W
    start = np.clip(col - NA_COLS // 2, 0, GRID_W - NA_COLS)[:, None]
    key_col = (GRID_W - 1 - np.arange(S) % GRID_W)[None]
    mask = np.where((key_col >= start) & (key_col < start + NA_COLS), 0, -BIG).astype(np.float32)
    return np.eye(P, dtype=np.float32), mask, onehot, lncount


def weight_stream(w):
    import numpy as np
    stream = np.empty((DEPTH * UNITS, P, UCOLS), np.float32)
    for l in range(DEPTH):
        at = l * UNITS

        def rows(m, a):
            return m[a * 512:(a + 1) * 512].reshape(4, P, 512).transpose(1, 0, 2).reshape(P, UCOLS)

        def ffn(u, w1, w3, w2):
            def up(c, a):
                cols = slice(c * FC, (c + 1) * FC)
                return rows(np.concatenate([w1[:, cols], w3[:, cols]], 1), a)

            def down(c):
                return w2[c * FC:(c + 1) * FC].reshape(2, P, D).transpose(1, 0, 2).reshape(P, UCOLS)

            units = [up(0, 0), up(0, 1)]
            for c in range(1, CHUNKS):
                units += [up(c, 0), up(c, 1), down(c - 1)]
            for k, m in enumerate(units + [down(CHUNKS - 1)]):
                stream[at + u + k] = m

        ffn(U_FFN1, w["w1_ff1"][l], w["w3_ff1"][l], w["w2_ff1"][l])
        ffn(U_FFN2, w["w1_ff2"][l], w["w3_ff2"][l], w["w2_ff2"][l])
        w_in, u = w["w_in"][l], at + U_QKV
        first = {BA: 0, BB: 3 * HEADS_W, BC: 6 * HEADS_W}
        for b in (BC, BB, BA):
            for c in range(3):
                for a in range(2):
                    c0 = first[b] + c * HEADS_W
                    stream[u] = rows(w_in[:, c0:c0 + HEADS_W], a)
                    u += 1
        which = {BA: 0, BB: 1, BC: 2}
        for kind, b, n, a in MIX:
            if kind == "gate":
                c0 = 9 * HEADS_W + which[b] * D + n * 512
                stream[u] = rows(w_in[:, c0:c0 + 512], a)
            else:
                stream[u] = rows(w["w_br_" + "abc"[which[b]]][l][:, n * 512:(n + 1) * 512], 0)
            u += 1
        for n in range(2):
            for a in range(2):
                stream[u] = rows(w["w_o"][l][:, n * 512:(n + 1) * 512], a)
                u += 1
    return stream


def kernel(**inputs):
    import numpy as np
    import concourse.bacc as bacc
    from concourse import mybir as mb
    from concourse.bass_utils import run_bass_kernel_spmd

    w = {k: np.asarray(a) for k, a in inputs.items()}
    gains = np.stack([w["g_ff1"], w["g_mix"], w["g_ff2"]], 1).reshape(DEPTH, 3 * KC, P)
    params = np.concatenate([gains, w["subln_g"][:, None]], 1).transpose(2, 0, 1)
    lam = np.stack([w["lam_q1"], w["lam_k1"], w["lam_q2"], w["lam_k2"]], 1)
    rpb = np.zeros((DEPTH, B_HEADS, RPB_ROWS, RPB_PITCH), np.float32)
    rpb[..., 48:48 + 2 * NA_COLS - 1] = w["na_rpb"][:, :, ::-1, ::-1]
    eye, mask, onehot, lncount = shape_constants()
    arrays = {"x": w["x"], "stream": weight_stream(w), "params": params, "lam": lam, "g_final": w["g_final"],
              "t5_table": w["t5_table"], "rpb": rpb, "ident": eye, "mask": mask, "onehot": onehot, "lncount": lncount}
    nc = bacc.Bacc("TRN2", target_bir_lowering=False, num_devices=1)
    feed, args = {}, []
    for name, a in arrays.items():
        a = np.ascontiguousarray(a)
        feed["in_" + name] = a
        args.append(nc.dram_tensor("in_" + name, a.shape, mb.dt.from_np(a.dtype), kind="ExternalInput").ap())
    args.append(nc.dram_tensor("out_y", (1, S, D), mb.dt.float32, kind="ExternalOutput").ap())
    build(nc, *args)
    r = run_bass_kernel_spmd(nc, [feed], core_ids=[0])
    return r.results[0]["out_y"]
```

```python
from contextlib import ExitStack
import math

import concourse.bass as bass
from concourse import mybir

F32 = mybir.dt.float32
F32R = mybir.dt.float32r
ALU = mybir.AluOpType
ACT = mybir.ActivationFunctionType

P = 128
D = 1024
S = 256
DEPTH = 2
DFF = 2816
TILES = S // P
KC = D // P
FC = 256
CHUNKS = DFF // FC
DH = 64
HEADS_W = 512
BLK = HEADS_W // P
A_HEADS, B_HEADS, C_HEADS = 4, 8, 8
GRID_W, NA_COLS, NA_ROWS = 64, 16, 8
EPS = 1e-6
BIG = 1e30
BC, BB, BA = 0, 1, 2
UCOLS = 2048
SLOTS = 3
CREDIT = 3
NEXT = 4

U_FFN1 = 0
U_QKV = 3 * CHUNKS
U_MIX = U_QKV + 18
MIX = ([("gate", BC, n, a) for n in range(2) for a in range(2)] + [("gate", BB, n, a) for n in range(2) for a in range(2)]
       + [("br", BC, n, 0) for n in range(2)] + [("gate", BA, n, a) for n in range(2) for a in range(2)]
       + [("br", BB, n, 0) for n in range(2)] + [("br", BA, n, 0) for n in range(2)])
U_WO = U_MIX + len(MIX)
U_FFN2 = U_WO + 4
UNITS = U_FFN2 + 3 * CHUNKS
PASSED_OVER = (U_MIX + 3, U_MIX + 9)
assert (UNITS + len(PASSED_OVER)) % SLOTS == 0
PAIRS = 12
OT_AT = {4: [(BC, 0)], 6: [(BC, 1)], 10: [(BB, 0)], 11: [(BB, 1)], 14: [(BA, 0), (BA, 1)]}
G_FF1, G_MIX, G_FF2, G_NEXT, SUBLN, NEGLAM, NPAR = 0, 8, 16, 24, 32, 33, 34
T5_HEADS = A_HEADS + C_HEADS
GRID_H = S // GRID_W
assert (UNITS - U_WO - 1) % SLOTS == 0 and U_MIX % SLOTS == 0
RPB_ROWS, RPB_PITCH = TILES * GRID_H, 128
QUARTERS_AT = {len(MIX) - 1: [(2, 0), (2, 1)], len(MIX): [(2, 2), (2, 3)], len(MIX) + 2: [(3, 0)], len(MIX) + 3: [(3, 1)]}


def lam_init(l):
    return 0.8 - 0.6 * math.exp(-0.3 * l)


def slot_of(u):
    u %= UNITS
    return (u + sum(u >= p for p in PASSED_OVER)) % SLOTS


def before_in_slot(u):
    return next(v for v in range(u - 1, u - 2 * SLOTS, -1) if slot_of(v) == slot_of(u))


def split_at(u):
    def ready(v):
        return max(before_in_slot(w) for w in range(v - SLOTS, v + 1))

    return [v for v in range(u, u + 3 * SLOTS) if ready(v) == u]


PER_SLOT = [sum(slot_of(u) == s for u in range(UNITS)) for s in range(SLOTS)]


def bcast(ap, n):
    return bass.AP(ap.tensor, ap.offset, [list(ap.ap[0]), list(ap.ap[-1]), [0, n]])


def build(nc, x_in, stream, params_in, lam_in, g_final, t5_table, rpb, c_ident, c_mask, c_onehot, c_lncount, out):
    with ExitStack() as ctx:
        def sb(name, shape, dt=F32):
            return ctx.enter_context(nc.sbuf_tensor(name, shape, dt))

        def sem(name):
            return ctx.enter_context(nc.semaphore(name))

        raw = sb("raw", [P, SLOTS, UCOLS])
        whi = sb("whi", [P, SLOTS, UCOLS], F32R)
        wlo = sb("wlo", [P, SLOTS, UCOLS], F32R)
        x = sb("x", [P, TILES, D])
        xTh = sb("xTh", [P, KC, S], F32R)
        xTl = sb("xTl", [P, KC, S], F32R)
        nat = sb("nat", [P, 4, 512])
        silu = sb("silu", [P, TILES, FC])
        h = sb("h", [P, TILES, FC])
        hTh = sb("hTh", [P, 2, S], F32R)
        hTl = sb("hTl", [P, 2, S], F32R)
        hTh_last = sb("hTh_last", [P, 2, S], F32R)
        hTl_last = sb("hTl_last", [P, 2, S], F32R)
        qkT = sb("qkT", [P, 3, 2, BLK, S])
        pairh, pairl = hTh_last, hTl_last
        merged = qkT[:, BC, :, :, :].rearrange("p a b s -> p a (b s)")
        v = sb("v", [P, 3, TILES, HEADS_W])
        gate = sb("gate", [P, 2, TILES, D])
        bias = sb("bias", [P, 2, 2, TILES, S])
        sneg = sb("sneg", [P, 2, TILES, S])
        probs = sb("probs", [P, 2, TILES, S])
        pT = sb("pT", [P, 2, TILES, S])
        o = sb("o", [P, 2, TILES, HEADS_W])
        oTh = sb("oTh", [P, BLK, S], F32R)
        oTl = sb("oTl", [P, BLK, S], F32R)
        ident = sb("ident", [P, P])
        mask = sb("mask", [P, S])
        params = sb("params", [P, DEPTH, NPAR])
        gains = sb("gains", [P, SUBLN])
        mixp = sb("mixp", [P, 2])
        t5_sb = sb("t5_sb", [32, T5_HEADS])
        sumsq = sb("sumsq", [P, TILES])
        meansq = sb("meansq", [P, TILES])
        rstd = sb("rstd", [P, 3, TILES])
        negmax = sb("negmax", [P, 2, TILES])
        den = sb("den", [P, 2, TILES])
        rden = [sb(f"rden{i}", [P, 2, TILES]) for i in range(4)]
        lrden = sb("lrden", [P, TILES])
        factors = sb("factors", [P, 2, TILES])
        a_sumsq = sb("a_sumsq", [P, TILES, A_HEADS])
        a_meansq = sb("a_meansq", [P, TILES * A_HEADS])
        a_rstd = sb("a_rstd", [P, TILES * A_HEADS])
        junk = sb("junk", [P, TILES, P])
        tick = sb("tick", [P, 2])
        warm = sb("warm", [P, TILES])
        minus_half = sb("minus_half", [P, 8])
        base_e = sb("base_e", [P, DEPTH * 2])
        lam_dot = sb("lam_dot", [P, DEPTH * 2])
        lam_exp = sb("lam_exp", [P, DEPTH, 2])
        bank = [ctx.enter_context(nc.psum_tensor(f"bank{i}", [P, 512], F32)) for i in range(8)]
        t5_rows = nc.dram_tensor("t5_rows", [T5_HEADS, 512], F32, kind="Internal").ap()

        raw_landed = [sem(f"raw_landed{s}") for s in range(SLOTS)]
        x_landed = [sem(f"x_landed{t}") for t in range(TILES)]
        ident_landed, params_landed, const_landed, mask_landed, lam_landed, t5_stored, gfin_landed, out_stored = map(
            sem, ("ident_landed", "params_landed", "const_landed", "mask_landed", "lam_landed", "t5_stored", "gfin_landed", "out_stored"))
        bias_landed = [sem(f"bias_landed{i}") for i in range(2)]
        half_done, unit_used, quarter_turned, h_turned, qk_turned, scores_ready, probs_turned, pv_done, o_turned, t5_product, y_done = map(
            sem, ("half_done", "unit_used", "quarter_turned", "h_turned", "qk_turned", "scores_ready", "probs_turned",
                  "pv_done", "o_turned", "t5_product", "y_done"))
        hi_ready, quarter_hi, squared, silu_done, h_hi, qkv_out, gate_ready, exp_done, pT0_ready, o_hi, pair_hi = map(
            sem, ("hi_ready", "quarter_hi", "squared", "silu_done", "h_hi", "qkv_out", "gate_ready", "exp_done",
                  "pT0_ready", "o_hi", "pair_hi"))
        (unit_split, quarter_ready, quarter_scaled, quarter_split, meansq_ready, gains_ready, mixp_ready, pair_split, gated, h_split, qk_ready, biased,
         rden_ready, mixed, pT1_ready, o_ready, a_squared, a_mean, a_normed, o_split, branch_read,
         t5_biased, out_ready, a_premix, branch_added) = map(
            sem, ("unit_split", "quarter_ready", "quarter_scaled", "quarter_split", "meansq_ready", "gains_ready", "mixp_ready", "pair_split", "gated",
                  "h_split", "qk_ready", "biased", "rden_ready", "mixed", "pT1_ready", "o_ready", "a_squared", "a_mean",
                  "a_normed", "o_split", "branch_read", "t5_biased", "out_ready", "a_premix", "branch_added"))
        pool_pow, rstd_ready, a_rstd_ready, half_set, setup_done, lam_step, bias_masked = map(
            sem, ("pool_pow", "rstd_ready", "a_rstd_ready", "half_set", "setup_done", "lam_step", "bias_masked"))

        def n_unit(l, u, i=0):
            return l * UNITS + (u + 1) + i * SLOTS

        def n_quarter(l, inst, q):
            return l * 16 + (4 * inst + q + 1)

        def n_landed(l, u, i=0):
            s = slot_of(u)
            held = sum(slot_of(v) == s for v in range(u % UNITS + 1)) + (PER_SLOT[s] if u >= UNITS else 0)
            return (l * PER_SLOT[s] + i + held) * 16

        def n_scaled(l, inst, q):
            return l * 12 + (4 * (inst - (inst > 2)) + q + 1)

        def n_norm(l, j):
            return l * 3 + (j + 1)

        def n_chunk(l, f, c):
            return l * (2 * CHUNKS) + c + (f * CHUNKS + 1)

        def n_gated(l, f, c, t):
            return l * (4 * CHUNKS) + c * 2 + (2 * f * CHUNKS + t + 1)

        def n_probs_turned(l, s, m):
            return l * 20 + ((2 * s + m if s < 8 else 16 + s - 8) + 1)

        def n_branch(l, b, n, t):
            return l * 12 + (4 * b + 2 * n + t + 1)

        def n_bias(l, s):
            per = {BC: 2, BB: 2, BA: 1}
            return l * (16 * sum(per[q // 4] for q in range(s % 2, PAIRS, 2))) + 16 * sum(per[q // 4] for q in range(s % 2, s + 1, 2))

        def o_turns(b, half):
            return (bank[6] if (b, half) == (BA, 1) else bank[7])[:, :].rearrange("p (a b) -> p a b", a=2)

        def o_parts(b, half):
            w = slice(2 * half, 2 * half + 2)
            return (xTh[:, 4 + w.start:4 + w.stop, :], xTl[:, 4 + w.start:4 + w.stop, :]) if b == BA else (oTh[:, w, :], oTl[:, w, :])

        def product_banks(j):
            first = 2 if j > PAIRS + 2 and j % 2 else 0
            return [bank[first][:, :], bank[first + 1][:, :]]

        block = ctx.enter_context(nc.Block())

        @block.sync
        def _(sp):
            def load(l, u, i=0):
                sp.wait_ge(unit_split, n_unit(l, before_in_slot(u), i) + CREDIT)
                sp.dma_start(raw[:, slot_of(u), :], stream[l * UNITS + i * SLOTS + u, :, :]).then_inc(raw_landed[slot_of(u)], 16)

            sp.dma_start(ident[:, :], c_ident).then_inc(ident_landed, 16)
            load(0, 0)
            for t in range(TILES):
                sp.dma_start(x[:, t, :], x_in[0, t * P:(t + 1) * P, :]).then_inc(x_landed[t], 16)
            with sp.Fori(0, DEPTH) as l:
                with sp.Fori(0, (U_MIX - 3) // SLOTS) as i:
                    for u in range(1, 1 + SLOTS):
                        load(l, u, i)
                for u in range(U_MIX - 2, U_WO + 1):
                    load(l, u)
                with sp.Fori(0, (UNITS - U_WO - 1) // SLOTS) as i:
                    for u in range(U_WO + 1, U_WO + 1 + SLOTS):
                        load(l, u, i)
                load(l, UNITS)
            load(DEPTH, 1)
            sp.wait_ge(out_ready, 1)
            sp.dma_start(out[0, 0:P, :], nat[:, 0:2, :].rearrange("p a b -> p (a b)")).then_inc(out_stored, 16)
            sp.wait_ge(out_ready, 2)
            sp.dma_start(out[0, P:S, :], nat[:, 2:4, :].rearrange("p a b -> p (a b)")).then_inc(out_stored, 16)
            sp.wait_ge(out_stored, 32)

        @block.gpsimd
        def _(pool):
            pool.memset(minus_half[:, :], -0.5).then_inc(half_set, 1)
            pool.memset(factors[:, 0, :], 0.5).then_inc(half_set, 1)
            pool.memset(factors[:, 1, :], 0.125).then_inc(half_set, 1)
            pool.memset(base_e[:, :], math.e).then_inc(half_set, 1)
            pool.wait_ge(half_set, 4)
            pool.wait_ge(t5_biased, 1)
            pool.dma_start(t5_rows, v[0:T5_HEADS, 1, 0, :]).then_inc(t5_stored, 16)
            pool.wait_ge(lam_landed, 16)
            pairs = gate[:, 0, 0, 0:DEPTH * 4 * DH].rearrange("p (a b d) -> p a b d", b=2, d=DH)
            products = gate[:, 0, 1, 0:DEPTH * 2 * DH].rearrange("p (a d) -> p a d", d=DH)
            pool.tensor_tensor(products, pairs[:, :, 0, :], pairs[:, :, 1, :], ALU.mult).then_inc(lam_step, 1)
            width, step = DH, 1
            while width > 1:
                width //= 2
                pool.wait_ge(lam_step, step)
                dst = products[:, :, 0:width] if width > 1 else lam_dot[:, :].rearrange("p (a d) -> p a d", d=1)
                pool.tensor_tensor(dst, products[:, :, 0:width], products[:, :, width:2 * width], ALU.add).then_inc(lam_step, 1)
                step += 1
            pool.wait_ge(lam_step, step)
            pool.tensor_tensor(lam_exp[:, :, :].rearrange("p a b -> p (a b)"), base_e[:, :], lam_dot[:, :], ALU.pow).then_inc(lam_step, 1)
            step += 1
            for l in range(DEPTH):
                pool.wait_ge(lam_step, step)
                neglam = params[:, l, NEGLAM:NEGLAM + 1]
                pool.tensor_tensor(neglam, lam_exp[:, l, 1:2], lam_exp[:, l, 0:1], ALU.subtract).then_inc(lam_step, 1)
                step += 1
                pool.wait_ge(lam_step, step)
                pool.tensor_scalar(neglam, neglam, -lam_init(l), None, ALU.add).then_inc(setup_done, 1)
                subln = params[:, l, SUBLN:SUBLN + 1]
                pool.tensor_scalar(subln, subln, 1.0 - lam_init(l), None, ALU.mult).then_inc(setup_done, 1)
            pool.wait_ge(mask_landed, 16)

            def inverse_rms(l, j):
                pool.wait_ge(meansq_ready, n_norm(l, j))
                pool.tensor_tensor(rstd[:, 0, :], meansq[:, :], minus_half[:, 0:TILES], ALU.pow).then_inc(pool_pow, 1)
                pool.wait_ge(pool_pow, n_norm(l, j))
                one = rstd[:, 0, :]
                both = bass.AP(one.tensor, one.offset, [list(one.ap[0]), [0, 2], [1, TILES]])
                pool.tensor_tensor(rstd[:, 1:3, :], both, factors[:, :, :], ALU.mult).then_inc(rstd_ready, 1)

            with pool.Fori(0, DEPTH) as l:
                inverse_rms(l, 0)
                inverse_rms(l, 1)
                for s in range(4 * BB, 4 * BB + 4):
                    pool.wait_ge(bias_landed[s % 2], n_bias(l, s))
                    tiles = bias[:, s % 2, :, :, :].rearrange("p m t k -> p (m t) k")
                    every = bass.AP(mask[:, :].tensor, mask[:, :].offset, [list(mask[:, :].ap[0]), [0, 2 * TILES], [1, S]])
                    pool.tensor_tensor(tiles, tiles, every, ALU.add).then_inc(bias_masked, 1)
                pool.wait_ge(a_mean, l + 1)
                pool.tensor_tensor(a_rstd[:, :], a_meansq[:, :], minus_half[:, :], ALU.pow).then_inc(a_rstd_ready, 1)
                inverse_rms(l, 2)
            inverse_rms(DEPTH, 0)

        @block.scalar
        def _(act):
            act.dma_start(params[:, :, 0:NEGLAM], params_in).then_inc(params_landed, 16)
            act.dma_start(v[0:32, 0, 0, :], c_onehot).then_inc(const_landed, 16)
            act.dma_start(t5_sb[:, :], t5_table).then_inc(const_landed, 16)
            act.dma_start(v[0:T5_HEADS, 0, 1, :], c_lncount).then_inc(const_landed, 16)
            act.wait_ge(half_set, 3)
            act.activation(warm[:, :], factors[:, 0, :], ACT.Copy)

            def to_hi(l, u, i=0):
                s = slot_of(u)
                act.wait_ge(unit_used, n_unit(l, before_in_slot(u), i) + CREDIT)
                act.wait_ge(raw_landed[s], n_landed(l, u, i))
                act.activation(whi[:, s, :], raw[:, s, :], ACT.Copy).then_inc(hi_ready, 1)

            def quarter(l, inst, q):
                t, n = q % 2, q // 2
                dst = xTh[:, 4 * n:4 * n + 4, t * P:(t + 1) * P]
                if inst == 2:
                    act.wait_ge(quarter_turned, n_quarter(l, inst, q))
                    src = bank[6 + q % 2][:, :]
                else:
                    act.wait_ge(quarter_scaled, n_scaled(l, inst, q))
                    src = nat[:, q, :]
                act.activation(dst, src.rearrange("p (a b) -> p a b", a=4), ACT.Copy).then_inc(quarter_hi, 1)

            def squares(l, inst):
                for t in range(TILES):
                    act.wait_ge(quarter_ready, n_quarter(l, inst, 2 + t))
                    act.activation((probs, sneg)[t][:, :, :, :].rearrange("p a b c -> p (a b c)"), x[:, t, :], ACT.Square,
                                   accum_out=sumsq[:, t:t + 1]).then_inc(squared, 1)

            def h_to_hi(l, f, c, last=False):
                act.wait_ge(h_turned, n_chunk(l, f, c))
                act.activation((hTh_last if last else hTh)[:, :, :], bank[6][:, :].rearrange("p (a b) -> p a b", a=2), ACT.Copy).then_inc(h_hi, 1)

            def gates_silu(l, f, c, u, i=0):
                for t in range(TILES):
                    if t == 0:
                        act.wait_ge(half_done, n_unit(l, u, i))
                    else:
                        act.wait_ge(unit_used, n_unit(l, u, i) + CREDIT)
                    act.activation(silu[:, t, :], bank[4 + t][:, 0:FC], ACT.Silu, scale=rstd[:, 0, t:t + 1]).then_inc(silu_done, 1)

            def later_quarters(l, inst, u):
                squares(l, inst)
                quarter(l, inst, 2)
                quarter(l, inst, 3)
                to_hi(l, u)

            def ffn(l, f, u0, j, following):
                to_hi(l, u0 + 3)
                act.wait_ge(rstd_ready, n_norm(l, j))
                gates_silu(l, f, 0, u0 + 1)
                to_hi(l, u0 + 4)

                def chunk(c, u, i, last=False):
                    h_to_hi(l, f, c - 1)
                    to_hi(l, u + 3, i)
                    gates_silu(l, f, c, u + 1, i)
                    to_hi(l, u + 4, i)
                    if last:
                        h_to_hi(l, f, c, last=True)
                    to_hi(l, u + 5, i)

                chunk(1, u0 + 2, 0)
                with act.Fori(0, CHUNKS - 3) as i:
                    chunk(i + 2, u0 + 5, i)
                chunk(CHUNKS - 1, u0 + 3 * CHUNKS - 4, 0, last=True)
                quarter(l, following, 0)
                quarter(l, following, 1)

            def pair_to_hi(l, s):
                if s % 4 == 0:
                    act.wait_ge(qk_ready, l * 12 + s + 4 + 4)
                if s:
                    act.wait_ge(scores_ready, l * 24 + 2 * s)
                act.activation(pairh[:, :, :], qkT[:, s // 4, :, s % 4, :], ACT.Copy).then_inc(pair_hi, 1)

            def load_bias(l, s):
                b, blk, ring = s // 4, s % 4, s % 2
                if b == BB:
                    for half in range(2):
                        row = (half * B_HEADS + 2 * blk) * RPB_ROWS
                        src = bass.AP(rpb.tensor, row * RPB_PITCH, [[2 * B_HEADS * RPB_ROWS * RPB_PITCH, DEPTH], [1, GRID_W],
                                                                    [RPB_PITCH, 2 * RPB_ROWS], [1, GRID_W]])
                        act.dma_start(bias[64 * half:64 * half + 64, ring, :, :, :].rearrange("p m t (r c) -> p (m t r) c", c=GRID_W),
                                      src[l]).then_inc(bias_landed[ring], 16)
                    return
                for m in range(1 if b == BA else 2):
                    head = blk if b == BA else A_HEADS + 2 * blk + m
                    src = bass.AP(t5_rows.tensor, head * 512, [[1, P], [P, TILES], [1, S]])
                    act.dma_start(bias[:, ring, m, :, :], src).then_inc(bias_landed[ring], 16)

            to_hi(0, 0)
            quarter(-1, NEXT, 0)
            quarter(-1, NEXT, 1)
            to_hi(0, 1)
            act.dma_start(gate[:, 0, 0, 0:DEPTH * 4 * DH], bass.AP(lam_in.tensor, 0, [[0, P], [1, DEPTH * 4 * DH]])).then_inc(lam_landed, 16)
            act.dma_start(mask[:, :], c_mask).then_inc(mask_landed, 16)
            with act.Fori(0, DEPTH) as l:
                later_quarters(l, 0, U_FFN1 + 2)
                ffn(l, 0, U_FFN1, 0, 1)
                later_quarters(l, 1, U_QKV + 2)
                act.wait_ge(rstd_ready, n_norm(l, 1))

                def branch(b):
                    for c in range(3):
                        u = U_QKV + 2 * c
                        to_hi(l, u + 3, b * 2)
                        for t in range(TILES):
                            if t == 0:
                                act.wait_ge(half_done, n_unit(l, u + 1, b * 2))
                            else:
                                act.wait_ge(unit_used, n_unit(l, u + 1, b * 2) + CREDIT)
                            dst = v[:, b, t, :] if c == 2 else nat[:, 2 * c + t, :]
                            scale = rstd[:, 2, t:t + 1] if c == 0 else rstd[:, 0, t:t + 1]
                            act.activation(dst, bank[2 * c + t][:, :], ACT.Copy, scale=scale).then_inc(qkv_out, 1)
                        to_hi(l, u + 4, b * 2)

                branch(0)
                act.wait_ge(setup_done, 4)
                act.wait_ge(t5_stored, 16)
                load_bias(l, 0)
                load_bias(l, 1)
                pair_to_hi(l, 0)
                with act.Fori(1, 3) as b:
                    branch(b)
                for j in range(len(MIX) + 4):
                    u = U_MIX + j
                    kind, b, n, a = MIX[j] if j < len(MIX) else ("wo", 0, 0, 0)
                    if kind == "gate" and a == 1:
                        for t in range(TILES):
                            if t == 0:
                                act.wait_ge(half_done, n_unit(l, u))
                            else:
                                act.wait_ge(unit_used, n_unit(l, u) + CREDIT)
                            act.activation(gate[:, b % 2, t, n * 512:(n + 1) * 512], bank[t][:, :], ACT.Tanh,
                                           scale=rstd[:, 1, t:t + 1]).then_inc(gate_ready, 1)
                    if j < PAIRS - 1:
                        pair_to_hi(l, j + 1)
                    for inst, q in QUARTERS_AT.get(j, []):
                        quarter(l, inst, q)
                    for w in split_at(u):
                        if j < len(MIX) + 3:
                            to_hi(l, w)
                    if 1 <= j <= PAIRS:
                        act.wait_ge(probs_turned, n_probs_turned(l, j - 1, 0))
                        act.activation(pT[:, 0, :, :], bank[4][:, :].rearrange("p (a b) -> p a b", a=2),
                                       ACT.Copy).then_inc(pT0_ready, 1)
                    if j < PAIRS:
                        if j >= 1:
                            act.wait_ge(probs_turned, n_probs_turned(l, j - 1, 0 if j - 1 >= 8 else 1))
                        for m in range(2):
                            act.wait_ge(biased, l * 24 + 2 * j + m + 1)
                            for t in range(TILES):
                                e = act.activation(probs[:, m, t, ::-1], sneg[:, m, t, :], ACT.Exp, scale=-1.0,
                                                   bias=negmax[:, m, t:t + 1], accum_out=den[:, m, t:t + 1])
                            e.then_inc(exp_done, 1)
                    if j < PAIRS - 2:
                        load_bias(l, j + 2)
                    for b2, half in OT_AT.get(j, []):
                        act.wait_ge(o_turned, l * 6 + 2 * b2 + half + 1)
                        dst, src = o_parts(b2, half)[0], o_turns(b2, half)
                        act.activation(dst, src, ACT.Copy, **({"scale": mixp[:, 0:1]} if b2 == BA else {})).then_inc(o_hi, 1)
                later_quarters(l, 3, U_FFN2 + 2)
                ffn(l, 1, U_FFN2, 2, NEXT)
            act.dma_start(gate[:, 0, 0, :], bass.AP(g_final.tensor, 0, [[0, P], [1, D]])).then_inc(gfin_landed, 16)
            squares(DEPTH, 0)

        @block.tensor
        def _(pe):
            def three(dst, sh, sl, mh, ml, start, stop):
                pe.matmul(dst, sh, mh, start=start, stop=False)
                pe.matmul(dst, sh, ml, start=False, stop=False)
                return pe.matmul(dst, sl, mh, start=False, stop=stop)

            def unit_rows(l, u, i, th, tl, k0, dst, start, stop, before=(None, None), mid=None):
                s = slot_of(u)
                pe.wait_ge(unit_split, n_unit(l, u, i) + CREDIT)
                for t in range(TILES):
                    if t == 1 and mid:
                        mid()
                    if before[t]:
                        before[t]()
                    for k in range(4):
                        cols, w = slice(t * P, (t + 1) * P), slice(k * 512, (k + 1) * 512)
                        last = three(dst[t], th[:, k0 + k, cols], tl[:, k0 + k, cols], whi[:, s, w], wlo[:, s, w],
                                     start and k == 0, stop and k == 3)
                    last.then_inc(half_done if t == 0 else unit_used, 1)

            def turn_quarter(l, inst, q):
                t, n = q % 2, q // 2
                src = merged if inst == 2 else x
                pe.wait_ge(quarter_ready, n_quarter(l, inst, q))
                if q >= 2:
                    if inst == 2:
                        pe.wait_ge(quarter_split, n_quarter(l, inst, q - 2))
                    else:
                        pe.wait_ge(quarter_scaled, n_scaled(l, inst, q - 2))
                for k in range(4):
                    c = (4 * n + k) * P
                    last = pe.transpose(bank[6 + q % 2][:, k * P:(k + 1) * P], src[:, t, c:c + P], ident[:, :])
                last.then_inc(quarter_turned, 1)

            def split(l, inst, q):
                return lambda: pe.wait_ge(quarter_split, n_quarter(l, inst, q))

            def later_quarters(l, inst):
                def go():
                    turn_quarter(l, inst, 2)
                    turn_quarter(l, inst, 3)
                return go

            def ffn(l, f, u0, inst, following):
                ab = [bank[4][:, :], bank[5][:, :]]

                def up(c, u, i, a):
                    free = (lambda: pe.wait_ge(gated, n_gated(l, f, c - 1, 0)), lambda: pe.wait_ge(gated, n_gated(l, f, c - 1, 1)))
                    unit_rows(l, u, i, xTh, xTl, 4 * a, ab, a == 0, a == 1, before=free if a == 0 else (None, None))

                def turn_h(c):
                    pe.wait_ge(gated, n_gated(l, f, c, 1))
                    for t in range(TILES):
                        for j in range(2):
                            last = pe.transpose(bank[6][:, j * S + t * P:j * S + (t + 1) * P], h[:, t, j * P:(j + 1) * P], ident[:, :])
                    last.then_inc(h_turned, 1)

                def down(c, u, i, start, stop, before_last=False):
                    last_chunk = stop
                    s = slot_of(u)
                    th, tl = (hTh_last, hTl_last) if last_chunk else (hTh, hTl)
                    pe.wait_ge(unit_split, n_unit(l, u, i) + CREDIT)
                    pe.wait_ge(h_split, n_chunk(l, f, c))
                    for n in range(2):
                        for t in range(TILES):
                            for j in range(2):
                                cols, w = slice(t * P, (t + 1) * P), slice(j * D + n * 512, j * D + (n + 1) * 512)
                                last = three(bank[2 * n + t][:, :], th[:, j, cols], tl[:, j, cols], whi[:, s, w], wlo[:, s, w],
                                             start and j == 0, stop and j == 1)
                                if last_chunk and (n, t, j) == (1, 0, 0):
                                    turn_quarter(l, following, 1)
                            if last_chunk and t == 0:
                                last.then_inc(y_done, 1)
                        last.then_inc(half_done if n == 0 else unit_used, 1)
                        if last_chunk and n == 0:
                            turn_quarter(l, following, 0)
                        if n == 0 and before_last:
                            turn_h(CHUNKS - 1)

                unit_rows(l, u0, 0, xTh, xTl, 0, ab, True, False, before=(split(l, inst, 0), split(l, inst, 1)), mid=later_quarters(l, inst))
                unit_rows(l, u0 + 1, 0, xTh, xTl, 4, ab, False, True, before=(split(l, inst, 2), split(l, inst, 3)))

                def chunk(c, u, i, start=False, last=False):
                    up(c, u, i, 0)
                    turn_h(c - 1)
                    up(c, u + 1, i, 1)
                    down(c - 1, u + 2, i, start, False, before_last=last)

                chunk(1, u0 + 2, 0, start=True)
                with pe.Fori(0, CHUNKS - 3) as i:
                    chunk(i + 2, u0 + 5, i)
                chunk(CHUNKS - 1, u0 + 3 * CHUNKS - 4, 0, last=True)
                down(CHUNKS - 1, u0 + 3 * CHUNKS - 1, 0, False, True)

            pe.sem_inc(unit_used, CREDIT)
            pe.wait_ge(ident_landed, 16)
            for t in range(TILES):
                pe.wait_ge(x_landed[t], 16)
                turn_quarter(-1, NEXT, t)
            pe.wait_ge(const_landed, 48)
            pe.matmul(bank[3][0:T5_HEADS, :], t5_sb[:, :], v[0:32, 0, 0, :], start=True, stop=True).then_inc(t5_product, 1)

            with pe.Fori(0, DEPTH) as l:
                ffn(l, 0, U_FFN1, 0, 1)
                u = U_QKV

                def turn_qk(b, c):
                    pe.wait_ge(qkv_out, l * 18 + b * 6 + (2 * c + 2))
                    for m in range(2):
                        pe.wait_ge(qk_ready, l * 12 + b * 4 + (2 * c + m + 1 - 2 + 4))
                        for blk in (2 * m, 2 * m + 1):
                            for t in range(TILES):
                                last = pe.transpose(bank[6 + m][:, (blk % 2) * S + t * P:(blk % 2) * S + (t + 1) * P],
                                                    nat[:, 2 * c + t, blk * P:(blk + 1) * P], ident[:, :])
                        last.then_inc(qk_turned, 1)

                def branch(b, first=False):
                    for c in range(3):
                        dst = [bank[2 * c][:, :], bank[2 * c + 1][:, :]]
                        at_first = first and c == 0
                        unit_rows(l, u + 2 * c, b * 2, xTh, xTl, 0, dst, True, False, mid=later_quarters(l, 1) if at_first else None,
                                  before=(split(l, 1, 0), split(l, 1, 1)) if at_first else (None, None))
                        if c:
                            turn_qk(b, c - 1)
                        unit_rows(l, u + 2 * c + 1, b * 2, xTh, xTl, 4, dst, False, True,
                                  before=(split(l, 1, 2), split(l, 1, 3)) if at_first else (None, None))

                branch(0, first=True)
                with pe.Fori(1, 3) as b:
                    branch(b)
                def scores(s):
                    b = s // 4
                    pe.wait_ge(pair_split, l * 12 + s + 1)
                    if s == 0:
                        pe.wait_ge(qkv_out, l * 18 + 18)
                    for t in range(TILES):
                        for m in range(2):
                            if s and t == 0:
                                pe.wait_ge(biased, l * 24 + 2 * (s - 1) + m + 1)
                            rows = slice(DH * m, DH * m + DH)
                            dst = bank[2 + m][:, t * S:(t + 1) * S]
                            cols = slice(t * P, (t + 1) * P)
                            last = three(dst, pairh[rows, 0, cols], pairl[rows, 0, cols], pairh[rows, 1, :], pairl[rows, 1, :],
                                         True, True)
                            if t == 1:
                                last.then_inc(scores_ready, 1)

                def turn_probs(s):
                    b = s // 4
                    if s:
                        pe.wait_ge(pT0_ready, l * 12 + s)
                        if s <= 8:
                            pe.wait_ge(pT1_ready, l * 8 + s)
                    for m in range(1 if b == BA else 2):
                        if b == BA:
                            pe.wait_ge(mixed, l * 4 + (s - 8) + 1)
                        else:
                            pe.wait_ge(exp_done, l * 24 + 2 * s + m + 1)
                        for kb in range(TILES):
                            for t in range(TILES):
                                last = pe.transpose(bank[4 + m][:, kb * S + t * P:kb * S + (t + 1) * P],
                                                    probs[:, m, t, kb * P:(kb + 1) * P], ident[:, :])
                        last.then_inc(probs_turned, 1)

                def values(s):
                    b, blk = s // 4, s % 4
                    pe.wait_ge(pT0_ready, l * 12 + s + 1)
                    if b != BA:
                        pe.wait_ge(pT1_ready, l * 8 + s + 1)
                    if s:
                        pe.wait_ge(o_ready, l * 12 + s)
                    maps, w = (1, P) if b == BA else (2, DH)
                    for t in range(TILES):
                        for m in range(maps):
                            c = blk * P + m * DH
                            for kb in range(TILES):
                                last = pe.matmul(bank[6][:, t * P + m * DH:t * P + m * DH + w], pT[:, m, kb, t * P:(t + 1) * P],
                                                 v[:, b, kb, c:c + w], start=kb == 0, stop=kb == 1)
                    last.then_inc(pv_done, 1)

                def turn_o(b, half):
                    if b == BA:
                        pe.wait_ge(a_normed, l + 1)
                    else:
                        pe.wait_ge(o_ready, l * 12 + 4 * b + 2 * half + 2)
                    if 2 * b + half and (b, half) != (BA, 1):
                        pe.wait_ge(o_split, l * 6 + 2 * b + half)
                    for k in range(2):
                        blk = 2 * half + k
                        for t in range(TILES):
                            last = pe.transpose(o_turns(b, half)[:, k, t * P:(t + 1) * P], o[:, b % 2, t, blk * P:(blk + 1) * P],
                                                ident[:, :])
                    last.then_inc(o_turned, 1)

                def products_read(j):
                    if j == PAIRS + 3:
                        return (None, None)
                    kind, b, n, _ = MIX[j - 1 if j < PAIRS + 3 else j - 2]
                    ready = gate_ready if kind == "gate" else branch_read
                    return tuple((lambda t=t: pe.wait_ge(ready, n_branch(l, b, n, t))) for t in range(TILES))

                for j, (kind, b, n, a) in enumerate(MIX):
                    pr = product_banks(j)
                    before = products_read(j) if j and a == 0 else (None, None)
                    if kind == "gate":
                        unit_rows(l, U_MIX + j, 0, xTh, xTl, 4 * a, pr, a == 0, a == 1, before=before)
                    else:
                        if n == 0:
                            pe.wait_ge(o_split, l * 6 + 2 * b + 2)
                        th, tl, k0 = (xTh, xTl, 4) if b == BA else (oTh, oTl, 0)
                        turn_first = (lambda: turn_quarter(l, 2, 0)) if (b, n) == (BA, 1) else None
                        unit_rows(l, U_MIX + j, 0, th, tl, k0, pr, True, True, before=before, mid=turn_first)
                    if j < PAIRS:
                        scores(j)
                    if 2 <= j < PAIRS + 2:
                        values(j - 2)
                    if 1 <= j <= PAIRS:
                        turn_probs(j - 1)
                    for b2, half in OT_AT.get(j, []):
                        turn_o(b2, half)
                turn_quarter(l, 2, 1)

                def y_free(n, a, t):
                    def go():
                        if n == 0:
                            pe.wait_ge(quarter_split, n_quarter(l, 2, 2 * a + t))
                        elif a == 0:
                            pe.wait_ge(branch_read, n_branch(l, BA, 1, t))
                    return go

                for n in range(2):
                    for a in range(2):
                        mid = later_quarters(l, 2) if n == a == 0 else (lambda: turn_quarter(l, 3, 1)) if n == a == 1 else None
                        if n == a == 1:
                            turn_quarter(l, 3, 0)
                        unit_rows(l, U_WO + 2 * n + a, 0, xTh, xTl, 4 * a, [bank[2 * n][:, :], bank[2 * n + 1][:, :]], a == 0, a == 1,
                                  before=(y_free(n, a, 0), y_free(n, a, 1)), mid=mid)
                ffn(l, 1, U_FFN2, 3, NEXT)

        @block.vector
        def _(dve):
            dve.sem_inc(unit_split, CREDIT)
            dve.sem_inc(qk_ready, 4)
            dve.sem_inc(quarter_ready, 4)
            dve.wait_ge(params_landed, 16)
            dve.tensor_copy(gains[:, :], params[:, DEPTH - 1, 0:SUBLN]).then_inc(gains_ready, 1)
            dve.wait_ge(gains_ready, 1)

            def to_lo(l, u, i=0):
                s = slot_of(u)
                dve.wait_ge(hi_ready, n_unit(l, u, i))
                dve.tensor_tensor(wlo[:, s, :], raw[:, s, :], whi[:, s, :].bitcast(F32), ALU.subtract).then_inc(unit_split, 1)

            def scale_quarter(l, inst, q):
                g = {0: G_FF1, 1: G_MIX, 3: G_FF2, NEXT: G_NEXT}[inst] + 4 * (q // 2)
                dve.wait_ge(quarter_turned, n_quarter(l, inst, q))
                dve.tensor_tensor(nat[:, q, :].rearrange("p (a b) -> p a b", a=4),
                                  bank[6 + q % 2][:, :].rearrange("p (a b) -> p a b", a=4),
                                  bcast(gains[:, g:g + 4], P), ALU.mult).then_inc(quarter_scaled, 1)

            def split_quarter(l, inst, q):
                t, n = q % 2, q // 2
                src = bank[6 + q % 2][:, :] if inst == 2 else nat[:, q, :]
                cols = (slice(None), slice(4 * n, 4 * n + 4), slice(t * P, (t + 1) * P))
                dve.wait_ge(quarter_hi, n_quarter(l, inst, q))
                dve.tensor_tensor(xTl[cols], src.rearrange("p (a b) -> p a b", a=4), xTh[cols].bitcast(F32),
                                  ALU.subtract).then_inc(quarter_split, 1)

            def two_quarters(l, inst, q):
                for k in (q, q + 1):
                    scale_quarter(l, inst, k)
                for k in (q, q + 1):
                    split_quarter(l, inst, k)

            def mean_squares(l, j):
                dve.wait_ge(squared, n_norm(l, j) * 2)
                dve.tensor_scalar(meansq[:, :], sumsq[:, :], 1.0 / D, EPS, ALU.mult, ALU.add).then_inc(meansq_ready, 1)

            def residual(q):
                t, n = q % 2, q // 2
                w = slice(n * 512, (n + 1) * 512)
                dve.scalar_tensor_tensor(out=x[:, t, w], in0=bank[q][:, :], scalar=0.5, in1=x[:, t, w], op0=ALU.mult,
                                         op1=ALU.add).then_inc(quarter_ready, 1)

            def h_to_lo(l, f, c, last=False):
                hi, lo = (hTh_last, hTl_last) if last else (hTh, hTl)
                dve.wait_ge(h_hi, n_chunk(l, f, c))
                dve.tensor_tensor(lo[:, :, :], bank[6][:, :].rearrange("p (a b) -> p a b", a=2), hi[:, :, :].bitcast(F32),
                                  ALU.subtract).then_inc(h_split, 1)

            def gated_h(l, f, c):
                for t in range(TILES):
                    dve.wait_ge(silu_done, n_gated(l, f, c, t))
                    dve.scalar_tensor_tensor(out=h[:, t, :], in0=bank[4 + t][:, FC:2 * FC], scalar=rstd[:, 0, t:t + 1],
                                             in1=silu[:, t, :], op0=ALU.mult, op1=ALU.mult).then_inc(gated, 1)

            def later_quarters(l, inst, j, u):
                if inst != 3:
                    to_lo(l, u - 1)
                two_quarters(l, inst, 2)
                mean_squares(l, j)
                to_lo(l, u)

            def ffn(l, f, u0, following):
                gated_h(l, f, 0)
                to_lo(l, u0 + 3)
                to_lo(l, u0 + 4)

                def chunk(c, u, i, last=False):
                    h_to_lo(l, f, c - 1)
                    to_lo(l, u + 3, i)
                    gated_h(l, f, c)
                    if last:
                        h_to_lo(l, f, c, last=True)
                    to_lo(l, u + 4, i)
                    if not last:
                        to_lo(l, u + 5, i)

                chunk(1, u0 + 2, 0)
                with dve.Fori(0, CHUNKS - 3) as i:
                    chunk(i + 2, u0 + 5, i)
                chunk(CHUNKS - 1, u0 + 3 * CHUNKS - 4, 0, last=True)
                u = u0 + 3 * CHUNKS - 1
                dve.wait_ge(y_done, l * 4 + 2 * f + 1)
                residual(0)
                dve.wait_ge(half_done, n_unit(l, u))
                residual(1)
                scale_quarter(l, following, 0)
                scale_quarter(l, following, 1)
                split_quarter(l, following, 0)
                dve.wait_ge(y_done, l * 4 + 2 * f + 2)
                residual(2)
                split_quarter(l, following, 1)
                dve.wait_ge(unit_used, n_unit(l, u) + CREDIT)
                residual(3)

            scale_quarter(-1, NEXT, 0)
            to_lo(0, 0)
            split_quarter(-1, NEXT, 0)
            scale_quarter(-1, NEXT, 1)
            split_quarter(-1, NEXT, 1)
            dve.wait_ge(t5_product, 1)
            dve.tensor_tensor(v[0:T5_HEADS, 1, 0, :], bank[3][0:T5_HEADS, :], v[0:T5_HEADS, 0, 1, :], ALU.add).then_inc(t5_biased, 1)
            with dve.Fori(0, DEPTH) as l:
                dve.tensor_copy(gains[:, :], params[:, l, 0:SUBLN]).then_inc(gains_ready, 1)
                dve.wait_ge(gains_ready, l + 2)
                later_quarters(l, 0, 0, U_FFN1 + 2)
                ffn(l, 0, U_FFN1, 1)
                later_quarters(l, 1, 1, U_QKV + 2)
                dve.wait_ge(setup_done, 4)
                dve.tensor_copy(mixp[:, :], params[:, l, SUBLN:NPAR]).then_inc(mixp_ready, 1)

                def pair_to_lo(s):
                    dve.wait_ge(pair_hi, l * 12 + s + 1)
                    dve.tensor_tensor(pairl[:, :, :], qkT[:, s // 4, :, s % 4, :], pairh[:, :, :].bitcast(F32),
                                      ALU.subtract).then_inc(pair_split, 1)

                def evacuate_qk(b, c):
                    for m in range(2):
                        dve.wait_ge(qk_turned, l * 12 + b * 4 + (2 * c + m + 1))
                        src = bank[6 + m][:, :].rearrange("p (a b) -> p a b", a=2)
                        dve.tensor_copy(qkT[:, b, c, 2 * m:2 * m + 2, :], src if c == 0 else src[:, :, ::-1]).then_inc(qk_ready, 1)

                def branch(b):
                    for c in range(3):
                        u = U_QKV + 2 * c
                        to_lo(l, u + 3, b * 2)
                        if c:
                            evacuate_qk(b, c - 1)
                        to_lo(l, u + 4, b * 2)

                branch(0)
                pair_to_lo(0)
                with dve.Fori(1, 3) as b:
                    branch(b)
                def add_branch(b, n, u):
                    w = slice(n * 512, (n + 1) * 512)
                    if (b, n) == (BA, 1):
                        split_quarter(l, 2, 0)
                    for t in range(TILES):
                        if t == 0:
                            dve.wait_ge(half_done, n_unit(l, u))
                        else:
                            dve.wait_ge(unit_used, n_unit(l, u) + CREDIT)
                        dve.wait_ge(gate_ready, n_branch(l, b, n, t))
                        dve.scalar_tensor_tensor(out=merged[:, t, w] if b == BC else nat[:, 2 * n + t, :],
                                                 in0=gate[:, b % 2, t, w], scalar=1.0, in1=product_banks(u - U_MIX)[t], op0=ALU.add,
                                                 op1=ALU.mult).then_inc(branch_read, 1)
                    if b == BC:
                        return
                    if (b, n) == (BA, 1):
                        split_quarter(l, 2, 1)
                    for t in range(TILES):
                        dve.wait_ge(branch_read, n_branch(l, b, n, t))
                        add = dve.tensor_tensor(merged[:, t, w], merged[:, t, w], nat[:, 2 * n + t, :], ALU.add)
                        add.then_inc(quarter_ready if b == BA else branch_added, 1)

                def add_bias(s):
                    b, ring = s // 4, s % 2
                    if b == BB:
                        dve.wait_ge(bias_masked, l * 4 + (s - 4 * BB + 1))
                    else:
                        dve.wait_ge(bias_landed[ring], n_bias(l, s))
                    if s:
                        dve.wait_ge(exp_done, l * 24 + 2 * s)
                    for m in range(2):
                        dve.wait_ge(scores_ready, l * 24 + 2 * s + m + 1)
                        dve.memset(tick[:, m:m + 1], 0.0)
                        for t in range(TILES):
                            r = dve.tensor_tensor_reduce(out=sneg[:, m, t, :], in0=bank[2 + m][:, t * S:(t + 1) * S],
                                                         in1=bias[:, ring, 0 if b == BA else m, t, :], scale=-1.0, scalar=3e38,
                                                         op0=ALU.add, op1=ALU.min, accum_out=negmax[:, m, t:t + 1])
                        r.then_inc(biased, 1)

                def split_o(j):
                    for b2, half in OT_AT.get(j, []):
                        hi, lo = o_parts(b2, half)
                        dve.wait_ge(o_hi, l * 6 + 2 * b2 + half + 1)
                        dve.scalar_tensor_tensor(out=lo, in0=o_turns(b2, half), scalar=mixp[:, 0:1] if b2 == BA else 1.0,
                                                 in1=hi.bitcast(F32), op0=ALU.mult, op1=ALU.subtract).then_inc(o_split, 1)

                def read_values(s):
                    b, blk = s // 4, s % 4
                    dve.wait_ge(pv_done, l * 12 + s + 1)
                    if b == BA:
                        dst = o[:, 0, :, blk * P:(blk + 1) * P]
                        dve.tensor_copy(dst, bank[6][:, 0:2 * P].rearrange("p (a b) -> p a b", a=2)).then_inc(o_ready, 1)
                        dve.wait_ge(o_ready, l * 12 + s + 1)
                        for t in range(TILES):
                            r = dve.tensor_tensor_reduce(out=junk[:, t, :], in0=o[:, 0, t, blk * P:(blk + 1) * P],
                                                         in1=o[:, 0, t, blk * P:(blk + 1) * P], scale=1.0, scalar=0.0, op0=ALU.mult,
                                                         op1=ALU.add, accum_out=a_sumsq[:, t, blk:blk + 1])
                        r.then_inc(a_squared, 1)
                        return
                    dve.wait_ge(rden_ready, l * 12 + s + 1)
                    for m in range(2):
                        for t in range(TILES):
                            r = dve.tensor_scalar(o[:, b % 2, t, blk * P + m * DH:blk * P + (m + 1) * DH],
                                                  bank[6][:, t * P + m * DH:t * P + (m + 1) * DH], rden[s % 4][:, m, t:t + 1], None,
                                                  ALU.mult)
                    r.then_inc(o_ready, 1)

                for j in range(len(MIX) + 4):
                    u = U_MIX + j
                    kind, b, n, a = MIX[j] if j < len(MIX) else ("wo", 0, 0, 0)
                    if j == PAIRS + 2:
                        dve.wait_ge(a_rstd_ready, l + 1)
                        oa = o[:, 0, :, :].rearrange("p t (a b) -> p (t a) b", b=P)
                        dve.tensor_tensor(oa, oa, bcast(a_rstd[:, :], P), ALU.mult).then_inc(a_normed, 1)
                    if kind == "br":
                        add_branch(b, n, u)
                    if j < PAIRS:
                        add_bias(j)
                    if j < PAIRS - 1:
                        pair_to_lo(j + 1)
                    if 2 <= j < PAIRS + 2:
                        read_values(j - 2)
                    if j == PAIRS + 1:
                        dve.wait_ge(a_squared, l * 4 + 4)
                        dve.tensor_scalar(a_meansq[:, :], a_sumsq[:, :, :].rearrange("p a b -> p (a b)"), 1.0 / P, EPS, ALU.mult,
                                          ALU.add).then_inc(a_mean, 1)
                    if 1 <= j <= 8:
                        dve.wait_ge(probs_turned, n_probs_turned(l, j - 1, 1))
                        dve.tensor_copy(pT[:, 1, :, :], bank[5][:, :].rearrange("p (a b) -> p a b", a=2)).then_inc(pT1_ready, 1)
                    if j >= PAIRS:
                        split_o(j)
                    if j == len(MIX):
                        split_quarter(l, 2, 2)
                        split_quarter(l, 2, 3)
                    if j == len(MIX) + 2:
                        scale_quarter(l, 3, 0)
                        split_quarter(l, 3, 0)
                    if j < len(MIX) + 3:
                        for w in split_at(u):
                            to_lo(l, w)
                    if j < PAIRS:
                        split_o(j)
                    if j < PAIRS:
                        dve.wait_ge(exp_done, l * 24 + 2 * j + 2)
                        dve.reciprocal(rden[j % 4][:, :, :], den[:, :, :]).then_inc(rden_ready, 1)
                        if j >= 8:
                            r = rden[j % 4]
                            dve.wait_ge(rden_ready, l * 12 + j + 1)
                            dve.tensor_scalar(lrden[:, :], r[:, 1, :], mixp[:, 1:2], None, ALU.mult)
                            for t in range(TILES):
                                w = dve.tensor_scalar(probs[:, 0, t, :], probs[:, 0, t, :], r[:, 0, t:t + 1], None, ALU.mult)
                            w.then_inc(a_premix, 1)
                            dve.wait_ge(a_premix, l * 4 + (j - 8) + 1)
                            for t in range(TILES):
                                w = dve.scalar_tensor_tensor(out=probs[:, 0, t, :], in0=probs[:, 1, t, :], scalar=lrden[:, t:t + 1],
                                                             in1=probs[:, 0, t, :], op0=ALU.mult, op1=ALU.add)
                            w.then_inc(mixed, 1)
                    if j == len(MIX) + 1:
                        dve.wait_ge(half_done, n_unit(l, u))
                        residual(0)
                        dve.wait_ge(unit_used, n_unit(l, u) + CREDIT)
                        residual(1)
                    if j == len(MIX) + 3:
                        dve.wait_ge(half_done, n_unit(l, u))
                        residual(2)
                        scale_quarter(l, 3, 1)
                        split_quarter(l, 3, 1)
                        dve.wait_ge(unit_used, n_unit(l, u) + CREDIT)
                        residual(3)
                later_quarters(l, 3, 2, U_FFN2 + 2)
                ffn(l, 1, U_FFN2, NEXT)
            mean_squares(DEPTH, 0)
            dve.wait_ge(rstd_ready, n_norm(DEPTH, 0))
            dve.wait_ge(gfin_landed, 16)
            for t in range(TILES):
                dve.scalar_tensor_tensor(out=nat[:, 2 * t:2 * t + 2, :].rearrange("p a b -> p (a b)"), in0=x[:, t, :],
                                         scalar=rstd[:, 0, t:t + 1], in1=gate[:, 0, 0, :], op0=ALU.mult,
                                         op1=ALU.mult).then_inc(out_ready, 1)


def shape_constants():
    import numpy as np
    delta = 255 - np.arange(511)
    n = np.abs(delta)
    large = 8 + (np.log(np.maximum(n, 1).astype(np.float32) / 8) / math.log(1024 / 8) * 8).astype(np.int32)
    bucket = np.where(delta > 0, 16, 0) + np.where(n < 8, n, np.minimum(large, 15))
    onehot = np.zeros((32, 512), np.float32)
    onehot[bucket, np.arange(511)] = 1
    count = (n <= 64).astype(int) + (delta % 4 == 0) + (delta % 16 == 0)
    lncount = np.zeros((T5_HEADS, 512), np.float32)
    lncount[A_HEADS:, :511] = np.where(count > 0, np.log(np.maximum(count, 1)), -BIG)
    col = np.arange(P) % GRID_W
    start = np.clip(col - NA_COLS // 2, 0, GRID_W - NA_COLS)[:, None]
    key_col = (GRID_W - 1 - np.arange(S) % GRID_W)[None]
    mask = np.where((key_col >= start) & (key_col < start + NA_COLS), 0, -BIG).astype(np.float32)
    return np.eye(P, dtype=np.float32), mask, onehot, lncount


def weight_stream(w):
    import numpy as np
    stream = np.empty((DEPTH * UNITS + 2, P, UCOLS), np.float32)
    stream[DEPTH * UNITS:] = 0
    for l in range(DEPTH):
        at = l * UNITS

        def rows(m, a):
            return m[a * 512:(a + 1) * 512].reshape(4, P, 512).transpose(1, 0, 2).reshape(P, UCOLS)

        def ffn(u, w1, w3, w2):
            def up(c, a):
                cols = slice(c * FC, (c + 1) * FC)
                return rows(np.concatenate([w1[:, cols], w3[:, cols]], 1), a)

            def down(c):
                return w2[c * FC:(c + 1) * FC].reshape(2, P, D).transpose(1, 0, 2).reshape(P, UCOLS)

            units = [up(0, 0), up(0, 1)]
            for c in range(1, CHUNKS):
                units += [up(c, 0), up(c, 1), down(c - 1)]
            for k, m in enumerate(units + [down(CHUNKS - 1)]):
                stream[at + u + k] = m

        ffn(U_FFN1, w["w1_ff1"][l], w["w3_ff1"][l], w["w2_ff1"][l])
        ffn(U_FFN2, w["w1_ff2"][l], w["w3_ff2"][l], w["w2_ff2"][l])
        w_in, u = w["w_in"][l], at + U_QKV
        first = {BA: 0, BB: 3 * HEADS_W, BC: 6 * HEADS_W}
        for b in (BC, BB, BA):
            for c in range(3):
                for a in range(2):
                    c0 = first[b] + c * HEADS_W
                    stream[u] = rows(w_in[:, c0:c0 + HEADS_W], a)
                    u += 1
        which = {BA: 0, BB: 1, BC: 2}
        for kind, b, n, a in MIX:
            if kind == "gate":
                c0 = 9 * HEADS_W + which[b] * D + n * 512
                stream[u] = rows(w_in[:, c0:c0 + 512], a)
            else:
                stream[u] = rows(w["w_br_" + "abc"[which[b]]][l][:, n * 512:(n + 1) * 512], 0)
            u += 1
        for n in range(2):
            for a in range(2):
                stream[u] = rows(w["w_o"][l][:, n * 512:(n + 1) * 512], a)
                u += 1
    return stream


def kernel(**inputs):
    import numpy as np
    import concourse.bacc as bacc
    from concourse import mybir as mb
    from concourse.bass_utils import run_bass_kernel_spmd

    w = {k: np.asarray(a) for k, a in inputs.items()}
    following = np.roll(w["g_ff1"], -1, 0)
    gains = np.stack([w["g_ff1"], w["g_mix"], w["g_ff2"], following], 1).reshape(DEPTH, 4 * KC, P)
    params = np.concatenate([gains, w["subln_g"][:, None]], 1).transpose(2, 0, 1)
    lam = np.stack([w["lam_q1"], w["lam_k1"], w["lam_q2"], w["lam_k2"]], 1)
    rpb = np.zeros((DEPTH, 2, B_HEADS, TILES, GRID_H, RPB_PITCH), np.float32)
    for half in range(2):
        for t in range(TILES):
            first = GRID_H - 1 - (2 * t + half) + NA_ROWS - 1
            rpb[:, half, :, t, :, 48:48 + 2 * NA_COLS - 1] = w["na_rpb"][:, :, first:first - GRID_H:-1, ::-1]
    eye, mask, onehot, lncount = shape_constants()
    arrays = {"x": w["x"], "stream": weight_stream(w), "params": params, "lam": lam, "g_final": w["g_final"],
              "t5_table": w["t5_table"], "rpb": rpb, "ident": eye, "mask": mask, "onehot": onehot, "lncount": lncount}
    nc = bacc.Bacc("TRN2", target_bir_lowering=False, num_devices=1)
    feed, args = {}, []
    for name, a in arrays.items():
        a = np.ascontiguousarray(a)
        feed["in_" + name] = a
        args.append(nc.dram_tensor("in_" + name, a.shape, mb.dt.from_np(a.dtype), kind="ExternalInput").ap())
    args.append(nc.dram_tensor("out_y", (1, S, D), mb.dt.float32, kind="ExternalOutput").ap())
    build(nc, *args)
    r = run_bass_kernel_spmd(nc, [feed], core_ids=[0])
    return r.results[0]["out_y"]
```

```python
from contextlib import ExitStack
import math

import concourse.bass as bass
from concourse import mybir

F32 = mybir.dt.float32
F32R = mybir.dt.float32r
ALU = mybir.AluOpType
ACT = mybir.ActivationFunctionType

P = 128
D = 1024
S = 256
DEPTH = 2
DFF = 2816
TILES = S // P
KC = D // P
FC = 256
CHUNKS = DFF // FC
DH = 64
HEADS_W = 512
BLK = HEADS_W // P
A_HEADS, B_HEADS, C_HEADS = 4, 8, 8
GRID_W, NA_COLS, NA_ROWS = 64, 16, 8
EPS = 1e-6
BIG = 1e30
BC, BB, BA = 0, 1, 2
UCOLS = 2048
SLOTS = 3
CREDIT = 3
NEXT = 4

U_FFN1 = 0
U_QKV = 3 * CHUNKS
U_MIX = U_QKV + 18
MIX = ([("gate", BC, n, a) for n in range(2) for a in range(2)] + [("gate", BB, n, a) for n in range(2) for a in range(2)]
       + [("br", BC, n, 0) for n in range(2)] + [("gate", BA, n, a) for n in range(2) for a in range(2)]
       + [("br", BB, n, 0) for n in range(2)] + [("br", BA, n, 0) for n in range(2)])
U_WO = U_MIX + len(MIX)
U_FFN2 = U_WO + 4
UNITS = U_FFN2 + 3 * CHUNKS
PASSED_OVER = (U_MIX + 3, U_MIX + 12)
assert (UNITS + len(PASSED_OVER)) % SLOTS == 0
PAIRS = 12
OT_AT = {4: [(BC, 0)], 6: [(BC, 1)], 9: [(BB, 0)], 10: [(BB, 1)], 14: [(BA, 0), (BA, 1)]}
G_FF1, G_MIX, G_FF2, G_NEXT, SUBLN, NEGLAM, NPAR = 0, 8, 16, 24, 32, 33, 34
T5_HEADS = A_HEADS + C_HEADS
GRID_H = S // GRID_W
assert (UNITS - U_WO - 1) % SLOTS == 0 and U_MIX % SLOTS == 0
RPB_ROWS, RPB_PITCH = TILES * GRID_H, 128
QUARTERS_AT = {len(MIX) - 1: [(2, 0), (2, 1)], len(MIX): [(2, 2), (2, 3)], len(MIX) + 2: [(3, 0)], len(MIX) + 3: [(3, 1)]}


def lam_init(l):
    return 0.8 - 0.6 * math.exp(-0.3 * l)


def slot_of(u):
    u %= UNITS
    return (u + sum(u >= p for p in PASSED_OVER)) % SLOTS


def before_in_slot(u):
    return next(v for v in range(u - 1, u - 2 * SLOTS, -1) if slot_of(v) == slot_of(u))


def split_at(u):
    def ready(v):
        return max(before_in_slot(w) for w in range(v - SLOTS, v + 1))

    return [v for v in range(u, u + 3 * SLOTS) if ready(v) == u]


PER_SLOT = [sum(slot_of(u) == s for u in range(UNITS)) for s in range(SLOTS)]


def map_columns(ap, other=False):
    return bass.AP(ap.tensor, ap.offset + (DH if other else 0), [list(ap.ap[0]), [S - DH if other else S + DH, 2], [P, TILES], [1, DH]])


def bcast(ap, n):
    return bass.AP(ap.tensor, ap.offset, [list(ap.ap[0]), list(ap.ap[-1]), [0, n]])


def build(nc, x_in, stream, params_in, lam_in, g_final, t5_table, rpb, c_ident, c_mask, c_onehot, c_lncount, out):
    with ExitStack() as ctx:
        def sb(name, shape, dt=F32):
            return ctx.enter_context(nc.sbuf_tensor(name, shape, dt))

        def sem(name):
            return ctx.enter_context(nc.semaphore(name))

        raw = sb("raw", [P, SLOTS, UCOLS])
        whi = sb("whi", [P, SLOTS, UCOLS], F32R)
        wlo = sb("wlo", [P, SLOTS, UCOLS], F32R)
        x = sb("x", [P, TILES, D])
        xTh = sb("xTh", [P, KC, S], F32R)
        xTl = sb("xTl", [P, KC, S], F32R)
        nat = sb("nat", [P, 4, 512])
        silu = sb("silu", [P, TILES, FC])
        pTa = silu
        h = sb("h", [P, TILES, FC])
        rms_row, rms_diag = h[:, 0, :], h[:, 1, :]
        ones = silu[:, 0, 0:P]
        hTh = sb("hTh", [P, 2, S], F32R)
        hTl = sb("hTl", [P, 2, S], F32R)
        vh, vl = hTh, hTl
        hTh_last = sb("hTh_last", [P, 2, S], F32R)
        hTl_last = sb("hTl_last", [P, 2, S], F32R)
        qkT = sb("qkT", [P, 3, 2, BLK, S])
        pairh, pairl = hTh_last, hTl_last
        merged = qkT[:, BC, :, :, :].rearrange("p a b s -> p a (b s)")
        v = sb("v", [P, 3, TILES, HEADS_W])
        gate = sb("gate", [P, 2, TILES, D])
        bias = sb("bias", [P, 2, 2, TILES, S])
        sneg = sb("sneg", [P, 2, TILES, S])
        probs = sb("probs", [P, 2, TILES, S])
        pTh = sb("pTh", [P, 2, TILES, S], F32R)
        pTl = sb("pTl", [P, 2, TILES, S], F32R)
        o = sb("o", [P, TILES, HEADS_W])
        oTh = sb("oTh", [P, BLK, S], F32R)
        oTl = sb("oTl", [P, BLK, S], F32R)
        ident = sb("ident", [P, P])
        mask = sb("mask", [P, S])
        params = sb("params", [P, DEPTH, NPAR])
        gains = sb("gains", [P, SUBLN])
        mixp = sb("mixp", [P, 2])
        t5_sb = sb("t5_sb", [32, T5_HEADS])
        sumsq = sb("sumsq", [P, TILES])
        meansq = sb("meansq", [P, TILES])
        rstd = sb("rstd", [P, 3, TILES])
        negmax = sb("negmax", [P, 2, TILES])
        den = sb("den", [P, 2, TILES])
        rden = [sb(f"rden{i}", [P, 2, TILES]) for i in range(2)]
        lrden = sb("lrden", [P, TILES])
        factors = sb("factors", [P, 2, TILES])
        a_sumsq = sb("a_sumsq", [P, TILES, A_HEADS])
        a_meansq = sb("a_meansq", [P, TILES * A_HEADS])
        a_rstd = sb("a_rstd", [P, TILES * A_HEADS])
        junk = sb("junk", [P, TILES, P])
        tick = sb("tick", [P, 2])
        warm = sb("warm", [P, TILES])
        minus_half = sb("minus_half", [P, 8])
        base_e = sb("base_e", [P, DEPTH * 2])
        lam_dot = sb("lam_dot", [P, DEPTH * 2])
        lam_exp = sb("lam_exp", [P, DEPTH, 2])
        bank = [ctx.enter_context(nc.psum_tensor(f"bank{i}", [P, 512], F32)) for i in range(8)]
        t5_rows = nc.dram_tensor("t5_rows", [T5_HEADS, 512], F32, kind="Internal").ap()

        raw_landed = [sem(f"raw_landed{s}") for s in range(SLOTS)]
        x_landed = [sem(f"x_landed{t}") for t in range(TILES)]
        ident_landed, params_landed, const_landed, mask_landed, lam_landed, t5_stored, gfin_landed, out_stored = map(
            sem, ("ident_landed", "params_landed", "const_landed", "mask_landed", "lam_landed", "t5_stored", "gfin_landed", "out_stored"))
        bias_landed = [sem(f"bias_landed{i}") for i in range(2)]
        half_done, unit_used, quarter_turned, h_turned, scores_ready, probs_turned, pv_done, o_turned, t5_product, y_done, row_product = map(
            sem, ("half_done", "unit_used", "quarter_turned", "h_turned", "scores_ready", "probs_turned",
                  "pv_done", "o_turned", "t5_product", "y_done", "row_product"))
        hi_ready, quarter_hi, squared, silu_done, h_hi, v_out, gate_ready, exp_done, pT_hi, v_hi, o_hi, pair_hi, out1_ready = map(
            sem, ("hi_ready", "quarter_hi", "squared", "silu_done", "h_hi", "v_out", "gate_ready", "exp_done",
                  "pT_hi", "v_hi", "o_hi", "pair_hi", "out1_ready"))
        (unit_split, quarter_ready, quarter_scaled, quarter_split, meansq_ready, gains_ready, mixp_ready, pair_split, diag_ready, row_ready, gated, h_split, qk_ready, biased,
         rden_ready, mixed, normed, pT_split, v_split, o_ready, a_squared, a_mean, a_normed, o_split, branch_read,
         t5_biased, out_ready, x_times_g, a_premix, branch_added) = map(
            sem, ("unit_split", "quarter_ready", "quarter_scaled", "quarter_split", "meansq_ready", "gains_ready", "mixp_ready", "pair_split", "diag_ready", "row_ready", "gated",
                  "h_split", "qk_ready", "biased", "rden_ready", "mixed", "normed", "pT_split", "v_split", "o_ready", "a_squared", "a_mean",
                  "a_normed", "o_split", "branch_read", "t5_biased", "out_ready", "x_times_g", "a_premix", "branch_added"))
        pool_pow, rstd_ready, a_rstd_ready, half_set, setup_done, lam_step, bias_masked, zeros_set, ones_set = map(
            sem, ("pool_pow", "rstd_ready", "a_rstd_ready", "half_set", "setup_done", "lam_step", "bias_masked", "zeros_set", "ones_set"))

        def n_unit(l, u, i=0):
            return l * UNITS + (u + 1) + i * SLOTS

        def n_quarter(l, inst, q):
            return l * 16 + (4 * inst + q + 1)

        def n_landed(l, u, i=0):
            s = slot_of(u)
            held = sum(slot_of(v) == s for v in range(u % UNITS + 1)) + (PER_SLOT[s] if u >= UNITS else 0)
            return (l * PER_SLOT[s] + i + held) * 16

        def n_scaled(l, inst, q):
            return l * 12 + (4 * (inst - (inst > 2)) + q + 1)

        def n_norm(l, j):
            return l * 3 + (j + 1)

        def n_chunk(l, f, c):
            return l * (2 * CHUNKS) + c + (f * CHUNKS + 1)

        def n_gated(l, f, c, t):
            return l * (4 * CHUNKS) + c * 2 + (2 * f * CHUNKS + t + 1)

        def n_probs_turned(l, s, m):
            return l * 20 + ((2 * s + m if s < 8 else 16 + s - 8) + 1)

        def n_branch(l, b, n, t):
            return l * 12 + (4 * b + 2 * n + t + 1)

        def n_bias(l, s):
            per = {BC: 2, BB: 2, BA: 1}
            return l * (16 * sum(per[q // 4] for q in range(s % 2, PAIRS, 2))) + 16 * sum(per[q // 4] for q in range(s % 2, s + 1, 2))

        def o_turns(b, half):
            return (bank[6] if (b == BA) == (half == 1) else bank[7])[:, :].rearrange("p (a b) -> p a b", a=2)

        def o_parts(b, half):
            w = slice(2 * half, 2 * half + 2)
            return (xTh[:, 4 + w.start:4 + w.stop, :], xTl[:, 4 + w.start:4 + w.stop, :]) if b == BA else (oTh[:, w, :], oTl[:, w, :])

        def v_of_pair(s):
            return v[:, s // 4, :, s % 4 * P:s % 4 * P + P].rearrange("p t (m d) -> p m t d", m=2)

        def product_banks(j):
            first = 2 if j > PAIRS + 2 and j % 2 else 0
            return [bank[first][:, :], bank[first + 1][:, :]]

        block = ctx.enter_context(nc.Block())

        @block.sync
        def _(sp):
            def load(l, u, i=0):
                sp.wait_ge(unit_split, n_unit(l, before_in_slot(u), i) + CREDIT)
                sp.dma_start(raw[:, slot_of(u), :], stream[l * UNITS + i * SLOTS + u, :, :]).then_inc(raw_landed[slot_of(u)], 16)

            def load_bias(l, s):
                b, blk, ring = s // 4, s % 4, s % 2
                if b == BB:
                    for half in range(2):
                        row = (half * B_HEADS + 2 * blk) * RPB_ROWS
                        src = bass.AP(rpb.tensor, row * RPB_PITCH, [[2 * B_HEADS * RPB_ROWS * RPB_PITCH, DEPTH], [1, GRID_W],
                                                                    [RPB_PITCH, 2 * RPB_ROWS], [1, GRID_W]])
                        sp.dma_start(bias[64 * half:64 * half + 64, ring, :, :, :].rearrange("p m t (r c) -> p (m t r) c", c=GRID_W),
                                      src[l]).then_inc(bias_landed[ring], 16)
                    return
                for m in range(1 if b == BA else 2):
                    head = blk if b == BA else A_HEADS + 2 * blk + m
                    src = bass.AP(t5_rows.tensor, head * 512, [[1, P], [P, TILES], [1, S]])
                    sp.dma_start(bias[:, ring, m, :, :], src).then_inc(bias_landed[ring], 16)

            sp.dma_start(ident[:, :], c_ident).then_inc(ident_landed, 16)
            load(0, 0)
            for t in range(TILES):
                sp.dma_start(x[:, t, :], x_in[0, t * P:(t + 1) * P, :]).then_inc(x_landed[t], 16)
            with sp.Fori(0, DEPTH) as l:
                with sp.Fori(0, (U_MIX - 3) // SLOTS) as i:
                    for u in range(1, 1 + SLOTS):
                        load(l, u, i)
                sp.wait_ge(t5_stored, 16)
                load_bias(l, 0)
                load_bias(l, 1)
                for u in range(U_MIX - 2, U_WO + 1):
                    s = u - U_MIX - 4
                    if 2 <= s < PAIRS:
                        sp.wait_ge(biased, l * 24 + 2 * (s - 2) + 2)
                        load_bias(l, s)
                    load(l, u)
                with sp.Fori(0, (UNITS - U_WO - 1) // SLOTS) as i:
                    for u in range(U_WO + 1, U_WO + 1 + SLOTS):
                        load(l, u, i)
                load(l, UNITS)
            load(DEPTH, 1)
            sp.wait_ge(out_ready, 1)
            sp.dma_start(out[0, 0:P, :], nat[:, 0:2, :].rearrange("p a b -> p (a b)")).then_inc(out_stored, 16)
            sp.wait_ge(out1_ready, 1)
            sp.dma_start(out[0, P:S, :], nat[:, 2:4, :].rearrange("p a b -> p (a b)")).then_inc(out_stored, 16)
            sp.wait_ge(out_stored, 32)

        @block.gpsimd
        def _(pool):
            pool.memset(minus_half[:, :], -0.5).then_inc(half_set, 1)
            pool.memset(factors[:, 0, :], 0.5).then_inc(half_set, 1)
            pool.memset(factors[:, 1, :], 0.125).then_inc(half_set, 1)
            pool.memset(base_e[:, :], math.e).then_inc(half_set, 1)
            pool.wait_ge(half_set, 4)
            pool.wait_ge(t5_biased, 1)
            pool.dma_start(t5_rows, v[0:T5_HEADS, 1, 0, :]).then_inc(t5_stored, 16)
            pool.wait_ge(lam_landed, 16)
            pairs = gate[:, 0, 0, 0:DEPTH * 4 * DH].rearrange("p (a b d) -> p a b d", b=2, d=DH)
            products = gate[:, 0, 1, 0:DEPTH * 2 * DH].rearrange("p (a d) -> p a d", d=DH)
            pool.tensor_tensor(products, pairs[:, :, 0, :], pairs[:, :, 1, :], ALU.mult).then_inc(lam_step, 1)
            width, step = DH, 1
            while width > 1:
                width //= 2
                pool.wait_ge(lam_step, step)
                dst = products[:, :, 0:width] if width > 1 else lam_dot[:, :].rearrange("p (a d) -> p a d", d=1)
                pool.tensor_tensor(dst, products[:, :, 0:width], products[:, :, width:2 * width], ALU.add).then_inc(lam_step, 1)
                step += 1
            pool.wait_ge(lam_step, step)
            pool.tensor_tensor(lam_exp[:, :, :].rearrange("p a b -> p (a b)"), base_e[:, :], lam_dot[:, :], ALU.pow).then_inc(lam_step, 1)
            step += 1
            for l in range(DEPTH):
                pool.wait_ge(lam_step, step)
                neglam = params[:, l, NEGLAM:NEGLAM + 1]
                pool.tensor_tensor(neglam, lam_exp[:, l, 1:2], lam_exp[:, l, 0:1], ALU.subtract).then_inc(lam_step, 1)
                step += 1
                pool.wait_ge(lam_step, step)
                pool.tensor_scalar(neglam, neglam, -lam_init(l), None, ALU.add).then_inc(setup_done, 1)
                subln = params[:, l, SUBLN:SUBLN + 1]
                pool.tensor_scalar(subln, subln, 1.0 - lam_init(l), None, ALU.mult).then_inc(setup_done, 1)
            pool.wait_ge(mask_landed, 16)

            def inverse_rms(l, j):
                pool.wait_ge(meansq_ready, n_norm(l, j))
                pool.tensor_tensor(rstd[:, 0, :], meansq[:, :], minus_half[:, 0:TILES], ALU.pow).then_inc(pool_pow, 1)
                pool.wait_ge(pool_pow, n_norm(l, j))
                one = rstd[:, 0, :]
                both = bass.AP(one.tensor, one.offset, [list(one.ap[0]), [0, 2], [1, TILES]])
                pool.tensor_tensor(rstd[:, 1:3, :], both, factors[:, :, :], ALU.mult).then_inc(rstd_ready, 1)

            with pool.Fori(0, DEPTH) as l:
                inverse_rms(l, 0)
                inverse_rms(l, 1)
                pool.memset(ones, 1.0).then_inc(ones_set, 1)
                for part in (vh, vl):
                    pool.memset(map_columns(part[:, :, :].bitcast(F32), other=True), 0.0).then_inc(zeros_set, 1)
                for s in range(4 * BB, 4 * BB + 4):
                    pool.wait_ge(bias_landed[s % 2], n_bias(l, s))
                    tiles = bias[:, s % 2, :, :, :].rearrange("p m t k -> p (m t) k")
                    every = bass.AP(mask[:, :].tensor, mask[:, :].offset, [list(mask[:, :].ap[0]), [0, 2 * TILES], [1, S]])
                    pool.tensor_tensor(tiles, tiles, every, ALU.add).then_inc(bias_masked, 1)
                pool.wait_ge(a_mean, l + 1)
                pool.tensor_tensor(a_rstd[:, :], a_meansq[:, :], minus_half[:, :], ALU.pow).then_inc(a_rstd_ready, 1)
                inverse_rms(l, 2)
            inverse_rms(DEPTH, 0)

        @block.scalar
        def _(act):
            act.dma_start(params[:, :, 0:NEGLAM], params_in).then_inc(params_landed, 16)
            act.dma_start(v[0:32, 0, 0, :], c_onehot).then_inc(const_landed, 16)
            act.dma_start(t5_sb[:, :], t5_table).then_inc(const_landed, 16)
            act.dma_start(v[0:T5_HEADS, 0, 1, :], c_lncount).then_inc(const_landed, 16)
            act.wait_ge(half_set, 3)
            act.activation(warm[:, :], factors[:, 0, :], ACT.Copy)

            def to_hi(l, u, i=0):
                s = slot_of(u)
                act.wait_ge(unit_used, n_unit(l, before_in_slot(u), i) + CREDIT)
                act.wait_ge(raw_landed[s], n_landed(l, u, i))
                act.activation(whi[:, s, :], raw[:, s, :], ACT.Copy).then_inc(hi_ready, 1)

            def quarter(l, inst, q):
                t, n = q % 2, q // 2
                dst = xTh[:, 4 * n:4 * n + 4, t * P:(t + 1) * P]
                if inst == 2:
                    act.wait_ge(quarter_turned, n_quarter(l, inst, q))
                    src = bank[6 + q % 2][:, :]
                else:
                    act.wait_ge(quarter_scaled, n_scaled(l, inst, q))
                    src = nat[:, q, :]
                act.activation(dst, src.rearrange("p (a b) -> p a b", a=4), ACT.Copy).then_inc(quarter_hi, 1)

            def squares(l, inst):
                for t in range(TILES):
                    act.wait_ge(quarter_ready, n_quarter(l, inst, 2 + t))
                    act.activation((probs, sneg)[t][:, :, :, :].rearrange("p a b c -> p (a b c)"), x[:, t, :], ACT.Square,
                                   accum_out=sumsq[:, t:t + 1]).then_inc(squared, 1)

            def h_to_hi(l, f, c, last=False):
                act.wait_ge(h_turned, n_chunk(l, f, c))
                act.activation((hTh_last if last else hTh)[:, :, :], bank[6][:, :].rearrange("p (a b) -> p a b", a=2), ACT.Copy).then_inc(h_hi, 1)

            def gates_silu(l, f, c, u, i=0):
                for t in range(TILES):
                    if t == 0:
                        act.wait_ge(half_done, n_unit(l, u, i))
                    else:
                        act.wait_ge(unit_used, n_unit(l, u, i) + CREDIT)
                    act.activation(silu[:, t, :], bank[4 + t][:, 0:FC], ACT.Silu, scale=rstd[:, 0, t:t + 1]).then_inc(silu_done, 1)

            def later_quarters(l, inst, u):
                squares(l, inst)
                quarter(l, inst, 2)
                quarter(l, inst, 3)
                to_hi(l, u)

            def ffn(l, f, u0, j, following):
                to_hi(l, u0 + 3)
                act.wait_ge(rstd_ready, n_norm(l, j))
                act.activation(warm[:, :], factors[:, 0, :], ACT.Silu)
                gates_silu(l, f, 0, u0 + 1)
                to_hi(l, u0 + 4)

                def chunk(c, u, i, last=False):
                    h_to_hi(l, f, c - 1)
                    to_hi(l, u + 3, i)
                    gates_silu(l, f, c, u + 1, i)
                    to_hi(l, u + 4, i)
                    if last:
                        h_to_hi(l, f, c, last=True)
                    to_hi(l, u + 5, i)

                chunk(1, u0 + 2, 0)
                with act.Fori(0, CHUNKS - 3) as i:
                    chunk(i + 2, u0 + 5, i)
                chunk(CHUNKS - 1, u0 + 3 * CHUNKS - 4, 0, last=True)
                quarter(l, following, 0)
                quarter(l, following, 1)

            def pair_to_hi(l, s):
                if s % 4 == 0:
                    act.wait_ge(qk_ready, l * 12 + s + 4)
                if s:
                    act.wait_ge(scores_ready, l * 24 + 2 * s)
                act.activation(pairh[:, :, :], qkT[:, s // 4, :, s % 4, :], ACT.Copy).then_inc(pair_hi, 1)

            to_hi(0, 0)
            quarter(-1, NEXT, 0)
            quarter(-1, NEXT, 1)
            to_hi(0, 1)
            act.dma_start(gate[:, 0, 0, 0:DEPTH * 4 * DH], bass.AP(lam_in.tensor, 0, [[0, P], [1, DEPTH * 4 * DH]])).then_inc(lam_landed, 16)
            act.dma_start(mask[:, :], c_mask).then_inc(mask_landed, 16)
            with act.Fori(0, DEPTH) as l:
                later_quarters(l, 0, U_FFN1 + 2)
                ffn(l, 0, U_FFN1, 0, 1)
                later_quarters(l, 1, U_QKV + 2)
                act.wait_ge(rstd_ready, n_norm(l, 1))

                def branch(b):
                    for p in range(3):
                        u = U_QKV + 2 * p
                        to_hi(l, u + 3, b * 2)
                        if p == 0:
                            for t in range(TILES):
                                if t == 0:
                                    act.wait_ge(half_done, n_unit(l, u + 1, b * 2))
                                else:
                                    act.wait_ge(unit_used, n_unit(l, u + 1, b * 2) + CREDIT)
                                act.activation(v[:, b, t, :], bank[t][:, :], ACT.Copy, scale=rstd[:, 0, t:t + 1]).then_inc(v_out, 1)
                        to_hi(l, u + 4, b * 2)

                branch(0)
                act.wait_ge(setup_done, 4)
                act.wait_ge(t5_stored, 16)
                pair_to_hi(l, 0)
                with act.Fori(1, 3) as b:
                    branch(b)
                act.activation(warm[:, :], factors[:, 0, :], ACT.Exp)
                for j in range(len(MIX) + 4):
                    u = U_MIX + j
                    kind, b, n, a = MIX[j] if j < len(MIX) else ("wo", 0, 0, 0)
                    if kind == "gate" and a == 1:
                        for t in range(TILES):
                            if t == 0:
                                act.wait_ge(half_done, n_unit(l, u))
                            else:
                                act.wait_ge(unit_used, n_unit(l, u) + CREDIT)
                            act.activation(gate[:, b % 2, t, n * 512:(n + 1) * 512], bank[t][:, :], ACT.Tanh,
                                           scale=rstd[:, 1, t:t + 1]).then_inc(gate_ready, 1)
                    if j < PAIRS - 1:
                        pair_to_hi(l, j + 1)
                    for inst, q in QUARTERS_AT.get(j, []):
                        quarter(l, inst, q)
                    due = split_at(u) if j < len(MIX) + 3 else []
                    for w in due[:1]:
                        to_hi(l, w)
                    if 1 <= j <= PAIRS:
                        for m in range(2 if j <= 8 else 1):
                            act.wait_ge(probs_turned, n_probs_turned(l, j - 1, m))
                            act.activation(pTh[:, m, :, :] if j <= 8 else pTa[:, :, :], bank[4 + m][:, :].rearrange("p (a b) -> p a b", a=2),
                                           ACT.Copy).then_inc(pT_hi, 1)
                    if 1 <= j <= 8:
                        if j > 1:
                            act.wait_ge(pv_done, l * 12 + j - 1)
                        act.activation(map_columns(vh[:, :, :]), v_of_pair(j - 1), ACT.Copy).then_inc(v_hi, 1)
                    if j < PAIRS:
                        if j >= 1:
                            act.wait_ge(probs_turned, n_probs_turned(l, j - 1, 0 if j - 1 >= 8 else 1))
                        for m in range(2):
                            act.wait_ge(biased, l * 24 + 2 * j + m + 1)
                            for t in range(TILES):
                                e = act.activation(probs[:, m, t, ::-1], sneg[:, m, t, :], ACT.Exp, scale=-1.0,
                                                   bias=negmax[:, m, t:t + 1], accum_out=den[:, m, t:t + 1])
                            e.then_inc(exp_done, 1)
                    for b2, half in OT_AT.get(j, []):
                        if b2 == BA:
                            act.wait_ge(o_turned, l * 2 + half + 1)
                        else:
                            act.wait_ge(pv_done, l * 12 + 4 * b2 + 2 * half + 2)
                        if b2 == BB:
                            act.wait_ge(unit_used, n_unit(l, U_MIX + 9) + CREDIT)
                        dst, src = o_parts(b2, half)[0], o_turns(b2, half)
                        act.activation(dst, src, ACT.Copy, **({"scale": mixp[:, 0:1]} if b2 == BA else {})).then_inc(o_hi, 1)
                    for w in due[1:]:
                        to_hi(l, w)
                later_quarters(l, 3, U_FFN2 + 2)
                ffn(l, 1, U_FFN2, 2, NEXT)
            act.dma_start(gate[:, 0, 0, :], bass.AP(g_final.tensor, 0, [[0, P], [1, D]])).then_inc(gfin_landed, 16)
            squares(DEPTH, 0)
            act.wait_ge(rstd_ready, n_norm(DEPTH, 0))
            act.wait_ge(x_times_g, 1)
            act.activation(nat[:, 2:4, :].rearrange("p a b -> p (a b)"), gate[:, 1, 0, :], ACT.Copy, scale=rstd[:, 0, 1:2]).then_inc(out1_ready, 1)

        @block.tensor
        def _(pe):
            def three(dst, sh, sl, mh, ml, start, stop):
                pe.matmul(dst, sh, mh, start=start, stop=False)
                pe.matmul(dst, sh, ml, start=False, stop=False)
                return pe.matmul(dst, sl, mh, start=False, stop=stop)

            def unit_rows(l, u, i, th, tl, k0, dst, start, stop, before=(None, None), mid=None):
                s = slot_of(u)
                pe.wait_ge(unit_split, n_unit(l, u, i) + CREDIT)
                for t in range(TILES):
                    if t == 1 and mid:
                        mid()
                    if before[t]:
                        before[t]()
                    for k in range(4):
                        cols, w = slice(t * P, (t + 1) * P), slice(k * 512, (k + 1) * 512)
                        last = three(dst[t], th[:, k0 + k, cols], tl[:, k0 + k, cols], whi[:, s, w], wlo[:, s, w],
                                     start and k == 0, stop and k == 3)
                    last.then_inc(half_done if t == 0 else unit_used, 1)

            def turn_quarter(l, inst, q):
                t, n = q % 2, q // 2
                src = merged if inst == 2 else x
                pe.wait_ge(quarter_ready, n_quarter(l, inst, q))
                if q >= 2:
                    if inst == 2:
                        pe.wait_ge(quarter_split, n_quarter(l, inst, q - 2))
                    else:
                        pe.wait_ge(quarter_scaled, n_scaled(l, inst, q - 2))
                for k in range(4):
                    c = (4 * n + k) * P
                    last = pe.transpose(bank[6 + q % 2][:, k * P:(k + 1) * P], src[:, t, c:c + P], ident[:, :])
                last.then_inc(quarter_turned, 1)

            def split(l, inst, q):
                return lambda: pe.wait_ge(quarter_split, n_quarter(l, inst, q))

            def later_quarters(l, inst):
                def go():
                    turn_quarter(l, inst, 2)
                    turn_quarter(l, inst, 3)
                return go

            def ffn(l, f, u0, inst, following):
                ab = [bank[4][:, :], bank[5][:, :]]

                def up(c, u, i, a):
                    free = (lambda: pe.wait_ge(gated, n_gated(l, f, c - 1, 0)), lambda: pe.wait_ge(gated, n_gated(l, f, c - 1, 1)))
                    unit_rows(l, u, i, xTh, xTl, 4 * a, ab, a == 0, a == 1, before=free if a == 0 else (None, None))

                def turn_h(c):
                    pe.wait_ge(gated, n_gated(l, f, c, 1))
                    for t in range(TILES):
                        for j in range(2):
                            last = pe.transpose(bank[6][:, j * S + t * P:j * S + (t + 1) * P], h[:, t, j * P:(j + 1) * P], ident[:, :])
                    last.then_inc(h_turned, 1)

                def down(c, u, i, start, stop, before_last=False):
                    last_chunk = stop
                    s = slot_of(u)
                    th, tl = (hTh_last, hTl_last) if last_chunk else (hTh, hTl)
                    pe.wait_ge(unit_split, n_unit(l, u, i) + CREDIT)
                    pe.wait_ge(h_split, n_chunk(l, f, c))
                    for n in range(2):
                        for t in range(TILES):
                            for j in range(2):
                                cols, w = slice(t * P, (t + 1) * P), slice(j * D + n * 512, j * D + (n + 1) * 512)
                                last = three(bank[2 * n + t][:, :], th[:, j, cols], tl[:, j, cols], whi[:, s, w], wlo[:, s, w],
                                             start and j == 0, stop and j == 1)
                                if last_chunk and (n, t, j) == (1, 0, 0):
                                    turn_quarter(l, following, 1)
                            if last_chunk and t == 0:
                                last.then_inc(y_done, 1)
                        last.then_inc(half_done if n == 0 else unit_used, 1)
                        if last_chunk and n == 0:
                            turn_quarter(l, following, 0)
                        if n == 0 and before_last:
                            turn_h(CHUNKS - 1)

                unit_rows(l, u0, 0, xTh, xTl, 0, ab, True, False, before=(split(l, inst, 0), split(l, inst, 1)), mid=later_quarters(l, inst))
                unit_rows(l, u0 + 1, 0, xTh, xTl, 4, ab, False, True, before=(split(l, inst, 2), split(l, inst, 3)))

                def chunk(c, u, i, start=False, last=False):
                    up(c, u, i, 0)
                    turn_h(c - 1)
                    up(c, u + 1, i, 1)
                    down(c - 1, u + 2, i, start, False, before_last=last)

                chunk(1, u0 + 2, 0, start=True)
                with pe.Fori(0, CHUNKS - 3) as i:
                    chunk(i + 2, u0 + 5, i)
                chunk(CHUNKS - 1, u0 + 3 * CHUNKS - 4, 0, last=True)
                down(CHUNKS - 1, u0 + 3 * CHUNKS - 1, 0, False, True)

            pe.sem_inc(unit_used, CREDIT)
            pe.wait_ge(ident_landed, 16)
            for t in range(TILES):
                pe.wait_ge(x_landed[t], 16)
                turn_quarter(-1, NEXT, t)
            pe.wait_ge(const_landed, 48)
            pe.matmul(bank[3][0:T5_HEADS, :], t5_sb[:, :], v[0:32, 0, 0, :], start=True, stop=True).then_inc(t5_product, 1)

            with pe.Fori(0, DEPTH) as l:
                ffn(l, 0, U_FFN1, 0, 1)
                u = U_QKV

                def unit_columns(u, i, k0, p, start, stop):
                    s = slot_of(u)
                    pe.wait_ge(unit_split, n_unit(l, u, i) + CREDIT)
                    for blk in range(BLK):
                        dst = bank[2 * p + blk // 2][:, blk % 2 * S:(blk % 2 + 1) * S]
                        for k in range(4):
                            w = slice(k * 512 + blk * P, k * 512 + (blk + 1) * P)
                            last = three(dst, whi[:, s, w], wlo[:, s, w], xTh[:, k0 + k, :], xTl[:, k0 + k, :],
                                         start and k == 0 and blk % 2 == 0, stop and k == 3 and blk % 2 == 1)
                        if blk == 1:
                            last.then_inc(half_done, 1)
                    last.then_inc(unit_used, 1)

                def branch(b, first=False):
                    dst = [bank[0][:, :], bank[1][:, :]]
                    if first:
                        unit_rows(l, u, 0, xTh, xTl, 0, dst, True, False, before=(split(l, 1, 0), split(l, 1, 1)), mid=later_quarters(l, 1))
                        unit_rows(l, u + 1, 0, xTh, xTl, 4, dst, False, True, before=(split(l, 1, 2), split(l, 1, 3)))
                        pe.wait_ge(ones_set, l + 1)
                        pe.wait_ge(diag_ready, l + 1)
                        for t in range(TILES):
                            w = slice(t * P, (t + 1) * P)
                            last = pe.matmul(bank[6][:, w], ones, rms_diag[:, w], start=True, stop=True)
                        last.then_inc(row_product, 1)
                    else:
                        pe.wait_ge(v_out, l * 6 + b * 2)
                        unit_rows(l, u, b * 2, xTh, xTl, 0, dst, True, False)
                        unit_rows(l, u + 1, b * 2, xTh, xTl, 4, dst, False, True)
                    for p in (1, 2):
                        if not first:
                            pe.wait_ge(qk_ready, l * 12 + b * 4 + (2 * p - 4))
                        unit_columns(u + 2 * p, b * 2, 0, p, True, False)
                        unit_columns(u + 2 * p + 1, b * 2, 4, p, False, True)

                branch(0, first=True)
                with pe.Fori(1, 3) as b:
                    branch(b)
                def scores(s):
                    b = s // 4
                    pe.wait_ge(pair_split, l * 12 + s + 1)
                    if s == 0:
                        pe.wait_ge(qk_ready, l * 12 + 12)
                    for t in range(TILES):
                        for m in range(2):
                            if s and t == 0:
                                pe.wait_ge(biased, l * 24 + 2 * (s - 1) + m + 1)
                            rows = slice(DH * m, DH * m + DH)
                            dst = bank[2 + m][:, t * S:(t + 1) * S]
                            cols = slice(t * P, (t + 1) * P)
                            last = three(dst, pairh[rows, 0, cols], pairl[rows, 0, cols], pairh[rows, 1, :], pairl[rows, 1, :],
                                         True, True)
                            if t == 1:
                                last.then_inc(scores_ready, 1)

                def turn_probs(s):
                    b = s // 4
                    if 1 <= s <= 8:
                        pe.wait_ge(pT_split, l * 16 + 2 * s)
                    elif s:
                        pe.wait_ge(pT_hi, n_probs_turned(l, s - 1, 0))
                    for m in range(1 if b == BA else 2):
                        if b == BA:
                            pe.wait_ge(mixed, l * 4 + (s - 8) + 1)
                        else:
                            pe.wait_ge(normed, l * 16 + 2 * s + m + 1)
                        for kb in range(TILES):
                            for t in range(TILES):
                                last = pe.transpose(bank[4 + m][:, kb * S + t * P:kb * S + (t + 1) * P],
                                                    probs[:, m, t, kb * P:(kb + 1) * P], ident[:, :])
                        last.then_inc(probs_turned, 1)

                def values(s):
                    b, blk = s // 4, s % 4
                    if b == BA:
                        pe.wait_ge(pT_hi, n_probs_turned(l, s, 0))
                        if s == 4 * BA:
                            pe.wait_ge(o_split, l * 6 + 2 * BB + 1)
                        else:
                            pe.wait_ge(o_ready, l * 4 + s - 4 * BA)
                        for t in range(TILES):
                            for kb in range(TILES):
                                last = pe.matmul(bank[6][:, t * P:(t + 1) * P], pTa[:, kb, t * P:(t + 1) * P],
                                                 v[:, b, kb, blk * P:(blk + 1) * P], start=kb == 0, stop=kb == 1)
                    else:
                        pe.wait_ge(pT_split, l * 16 + 2 * s + 2)
                        pe.wait_ge(v_split, l * 8 + s + 1)
                        if b == BB and blk % 2 == 0:
                            pe.wait_ge(o_split, l * 6 + blk // 2 + 1)
                        if s == 0:
                            pe.wait_ge(zeros_set, l * 2 + 2)
                        for m in range(2):
                            for kb in range(TILES):
                                w = slice(kb * P, (kb + 1) * P)
                                last = three(o_turns(b, blk // 2)[:, blk % 2, :], vh[:, m, w], vl[:, m, w], pTh[:, m, kb, :],
                                             pTl[:, m, kb, :], m == kb == 0, m == kb == 1)
                    last.then_inc(pv_done, 1)

                def turn_o(half):
                    pe.wait_ge(a_normed, l + 1)
                    if half == 0:
                        pe.wait_ge(o_split, l * 6 + 2 * BB + 2)
                    for k in range(2):
                        blk = 2 * half + k
                        for t in range(TILES):
                            last = pe.transpose(o_turns(BA, half)[:, k, t * P:(t + 1) * P], o[:, t, blk * P:(blk + 1) * P], ident[:, :])
                    last.then_inc(o_turned, 1)

                def products_read(j):
                    if j == PAIRS + 3:
                        return (None, None)
                    kind, b, n, _ = MIX[j - 1 if j < PAIRS + 3 else j - 2]
                    ready = gate_ready if kind == "gate" else branch_read
                    return tuple((lambda t=t: pe.wait_ge(ready, n_branch(l, b, n, t))) for t in range(TILES))

                pe.wait_ge(v_out, l * 6 + 6)
                for j, (kind, b, n, a) in enumerate(MIX):
                    pr = product_banks(j)
                    before = products_read(j) if j and a == 0 else (None, None)
                    if kind == "gate":
                        unit_rows(l, U_MIX + j, 0, xTh, xTl, 4 * a, pr, a == 0, a == 1, before=before)
                    else:
                        if n == 0:
                            pe.wait_ge(o_split, l * 6 + 2 * b + 2)
                        th, tl, k0 = (xTh, xTl, 4) if b == BA else (oTh, oTl, 0)
                        turn_first = (lambda: turn_quarter(l, 2, 0)) if (b, n) == (BA, 1) else None
                        unit_rows(l, U_MIX + j, 0, th, tl, k0, pr, True, True, before=before, mid=turn_first)
                    if j < PAIRS:
                        scores(j)
                    if 2 <= j < PAIRS + 2:
                        values(j - 2)
                    if 1 <= j <= PAIRS:
                        turn_probs(j - 1)
                    if j == PAIRS + 2:
                        turn_o(0)
                        turn_o(1)
                turn_quarter(l, 2, 1)

                def y_free(n, a, t):
                    def go():
                        if n == 0:
                            pe.wait_ge(quarter_split, n_quarter(l, 2, 2 * a + t))
                        elif a == 0:
                            pe.wait_ge(branch_read, n_branch(l, BA, 1, t))
                    return go

                for n in range(2):
                    for a in range(2):
                        mid = later_quarters(l, 2) if n == a == 0 else (lambda: turn_quarter(l, 3, 1)) if n == a == 1 else None
                        if n == a == 1:
                            turn_quarter(l, 3, 0)
                        unit_rows(l, U_WO + 2 * n + a, 0, xTh, xTl, 4 * a, [bank[2 * n][:, :], bank[2 * n + 1][:, :]], a == 0, a == 1,
                                  before=(y_free(n, a, 0), y_free(n, a, 1)), mid=mid)
                ffn(l, 1, U_FFN2, 3, NEXT)

        @block.vector
        def _(dve):
            dve.sem_inc(unit_split, CREDIT)
            dve.sem_inc(quarter_ready, 4)
            dve.wait_ge(params_landed, 16)
            dve.tensor_copy(gains[:, :], params[:, DEPTH - 1, 0:SUBLN]).then_inc(gains_ready, 1)
            dve.wait_ge(gains_ready, 1)

            def to_lo(l, u, i=0):
                s = slot_of(u)
                dve.wait_ge(hi_ready, n_unit(l, u, i))
                dve.tensor_tensor(wlo[:, s, :], raw[:, s, :], whi[:, s, :].bitcast(F32), ALU.subtract).then_inc(unit_split, 1)

            def scale_quarter(l, inst, q):
                g = {0: G_FF1, 1: G_MIX, 3: G_FF2, NEXT: G_NEXT}[inst] + 4 * (q // 2)
                dve.wait_ge(quarter_turned, n_quarter(l, inst, q))
                dve.tensor_tensor(nat[:, q, :].rearrange("p (a b) -> p a b", a=4),
                                  bank[6 + q % 2][:, :].rearrange("p (a b) -> p a b", a=4),
                                  bcast(gains[:, g:g + 4], P), ALU.mult).then_inc(quarter_scaled, 1)

            def split_quarter(l, inst, q):
                t, n = q % 2, q // 2
                src = bank[6 + q % 2][:, :] if inst == 2 else nat[:, q, :]
                cols = (slice(None), slice(4 * n, 4 * n + 4), slice(t * P, (t + 1) * P))
                dve.wait_ge(quarter_hi, n_quarter(l, inst, q))
                dve.tensor_tensor(xTl[cols], src.rearrange("p (a b) -> p a b", a=4), xTh[cols].bitcast(F32),
                                  ALU.subtract).then_inc(quarter_split, 1)

            def two_quarters(l, inst, q):
                for k in (q, q + 1):
                    scale_quarter(l, inst, k)
                for k in (q, q + 1):
                    split_quarter(l, inst, k)

            def mean_squares(l, j):
                dve.wait_ge(squared, n_norm(l, j) * 2)
                dve.tensor_scalar(meansq[:, :], sumsq[:, :], 1.0 / D, EPS, ALU.mult, ALU.add).then_inc(meansq_ready, 1)

            def residual(q):
                t, n = q % 2, q // 2
                w = slice(n * 512, (n + 1) * 512)
                dve.scalar_tensor_tensor(out=x[:, t, w], in0=bank[q][:, :], scalar=0.5, in1=x[:, t, w], op0=ALU.mult,
                                         op1=ALU.add).then_inc(quarter_ready, 1)

            def h_to_lo(l, f, c, last=False):
                hi, lo = (hTh_last, hTl_last) if last else (hTh, hTl)
                dve.wait_ge(h_hi, n_chunk(l, f, c))
                dve.tensor_tensor(lo[:, :, :], bank[6][:, :].rearrange("p (a b) -> p a b", a=2), hi[:, :, :].bitcast(F32),
                                  ALU.subtract).then_inc(h_split, 1)

            def gated_h(l, f, c):
                for t in range(TILES):
                    dve.wait_ge(silu_done, n_gated(l, f, c, t))
                    dve.scalar_tensor_tensor(out=h[:, t, :], in0=bank[4 + t][:, FC:2 * FC], scalar=rstd[:, 0, t:t + 1],
                                             in1=silu[:, t, :], op0=ALU.mult, op1=ALU.mult).then_inc(gated, 1)

            def later_quarters(l, inst, j, u):
                if inst != 3:
                    to_lo(l, u - 1)
                two_quarters(l, inst, 2)
                mean_squares(l, j)
                to_lo(l, u)

            def ffn(l, f, u0, following):
                gated_h(l, f, 0)
                to_lo(l, u0 + 3)
                to_lo(l, u0 + 4)

                def chunk(c, u, i, last=False):
                    h_to_lo(l, f, c - 1)
                    to_lo(l, u + 3, i)
                    gated_h(l, f, c)
                    if last:
                        h_to_lo(l, f, c, last=True)
                    to_lo(l, u + 4, i)
                    if not last:
                        to_lo(l, u + 5, i)

                chunk(1, u0 + 2, 0)
                with dve.Fori(0, CHUNKS - 3) as i:
                    chunk(i + 2, u0 + 5, i)
                chunk(CHUNKS - 1, u0 + 3 * CHUNKS - 4, 0, last=True)
                u = u0 + 3 * CHUNKS - 1
                dve.wait_ge(y_done, l * 4 + 2 * f + 1)
                residual(0)
                dve.wait_ge(half_done, n_unit(l, u))
                residual(1)
                scale_quarter(l, following, 0)
                scale_quarter(l, following, 1)
                split_quarter(l, following, 0)
                dve.wait_ge(y_done, l * 4 + 2 * f + 2)
                residual(2)
                split_quarter(l, following, 1)
                dve.wait_ge(unit_used, n_unit(l, u) + CREDIT)
                residual(3)

            scale_quarter(-1, NEXT, 0)
            to_lo(0, 0)
            split_quarter(-1, NEXT, 0)
            scale_quarter(-1, NEXT, 1)
            split_quarter(-1, NEXT, 1)
            dve.wait_ge(t5_product, 1)
            dve.tensor_tensor(v[0:T5_HEADS, 1, 0, :], bank[3][0:T5_HEADS, :], v[0:T5_HEADS, 0, 1, :], ALU.add).then_inc(t5_biased, 1)
            with dve.Fori(0, DEPTH) as l:
                dve.tensor_copy(gains[:, :], params[:, l, 0:SUBLN]).then_inc(gains_ready, 1)
                dve.wait_ge(gains_ready, l + 2)
                later_quarters(l, 0, 0, U_FFN1 + 2)
                ffn(l, 0, U_FFN1, 1)
                later_quarters(l, 1, 1, U_QKV + 2)
                dve.wait_ge(setup_done, 4)
                dve.tensor_copy(mixp[:, :], params[:, l, SUBLN:NPAR]).then_inc(mixp_ready, 1)

                def pair_to_lo(s):
                    dve.wait_ge(pair_hi, l * 12 + s + 1)
                    dve.tensor_tensor(pairl[:, :, :], qkT[:, s // 4, :, s % 4, :], pairh[:, :, :].bitcast(F32),
                                      ALU.subtract).then_inc(pair_split, 1)

                def evacuate_qk(b, c):
                    u = U_QKV + 2 * (c + 1) + 1
                    row = rms_row if c == 0 else rms_row[:, ::-1]
                    row = bass.AP(row.tensor, row.offset, [list(row.ap[0]), [0, 2], list(row.ap[-1])])
                    for m in range(2):
                        if m == 0:
                            dve.wait_ge(half_done, n_unit(l, u, b * 2))
                        else:
                            dve.wait_ge(unit_used, n_unit(l, u, b * 2) + CREDIT)
                        src = bank[2 * (c + 1) + m][:, :].rearrange("p (a b) -> p a b", a=2)
                        dve.scalar_tensor_tensor(out=qkT[:, b, c, 2 * m:2 * m + 2, :], in0=src if c == 0 else src[:, :, ::-1],
                                                 scalar=DH ** -0.5 if c == 0 else 1.0, in1=row, op0=ALU.mult,
                                                 op1=ALU.mult).then_inc(qk_ready, 1)

                dve.wait_ge(rstd_ready, n_norm(l, 1))
                for t in range(TILES):
                    r = dve.tensor_scalar(rms_diag[:, t * P:(t + 1) * P], ident[:, :], rstd[:, 0, t:t + 1], None, ALU.mult)
                r.then_inc(diag_ready, 1)

                def branch(b, first=False):
                    for p in range(3):
                        u = U_QKV + 2 * p
                        to_lo(l, u + 3, b * 2)
                        if first and p == 0:
                            dve.wait_ge(row_product, l + 1)
                            dve.tensor_copy(rms_row, bank[6][:, 0:S]).then_inc(row_ready, 1)
                            dve.wait_ge(row_ready, l + 1)
                        if p:
                            evacuate_qk(b, p - 1)
                        to_lo(l, u + 4, b * 2)

                branch(0, first=True)
                pair_to_lo(0)
                with dve.Fori(1, 3) as b:
                    branch(b)
                def add_branch(b, n, u):
                    w = slice(n * 512, (n + 1) * 512)
                    if (b, n) == (BA, 1):
                        split_quarter(l, 2, 0)
                    for t in range(TILES):
                        if t == 0:
                            dve.wait_ge(half_done, n_unit(l, u))
                        else:
                            dve.wait_ge(unit_used, n_unit(l, u) + CREDIT)
                        dve.wait_ge(gate_ready, n_branch(l, b, n, t))
                        dve.scalar_tensor_tensor(out=merged[:, t, w] if b == BC else nat[:, 2 * n + t, :],
                                                 in0=gate[:, b % 2, t, w], scalar=1.0, in1=product_banks(u - U_MIX)[t], op0=ALU.add,
                                                 op1=ALU.mult).then_inc(branch_read, 1)
                    if b == BC:
                        return
                    if (b, n) == (BA, 1):
                        split_quarter(l, 2, 1)
                    for t in range(TILES):
                        dve.wait_ge(branch_read, n_branch(l, b, n, t))
                        add = dve.tensor_tensor(merged[:, t, w], merged[:, t, w], nat[:, 2 * n + t, :], ALU.add)
                        add.then_inc(quarter_ready if b == BA else branch_added, 1)

                def add_bias(s):
                    b, ring = s // 4, s % 2
                    if b == BB:
                        dve.wait_ge(bias_masked, l * 4 + (s - 4 * BB + 1))
                    else:
                        dve.wait_ge(bias_landed[ring], n_bias(l, s))
                    if s:
                        dve.wait_ge(exp_done, l * 24 + 2 * s)
                    for m in range(2):
                        dve.wait_ge(scores_ready, l * 24 + 2 * s + m + 1)
                        dve.memset(tick[:, m:m + 1], 0.0)
                        for t in range(TILES):
                            r = dve.tensor_tensor_reduce(out=sneg[:, m, t, :], in0=bank[2 + m][:, t * S:(t + 1) * S],
                                                         in1=bias[:, ring, 0 if b == BA else m, t, :], scale=-1.0, scalar=3e38,
                                                         op0=ALU.add, op1=ALU.min, accum_out=negmax[:, m, t:t + 1])
                        r.then_inc(biased, 1)

                def split_o(j):
                    for b2, half in OT_AT.get(j, []):
                        hi, lo = o_parts(b2, half)
                        dve.wait_ge(o_hi, l * 6 + 2 * b2 + half + 1)
                        dve.scalar_tensor_tensor(out=lo, in0=o_turns(b2, half), scalar=mixp[:, 0:1] if b2 == BA else 1.0,
                                                 in1=hi.bitcast(F32), op0=ALU.mult, op1=ALU.subtract).then_inc(o_split, 1)

                def read_values(s):
                    w = slice((s - 4 * BA) * P, (s - 4 * BA + 1) * P)
                    dve.wait_ge(pv_done, l * 12 + s + 1)
                    dve.tensor_copy(o[:, :, w], bank[6][:, 0:2 * P].rearrange("p (a b) -> p a b", a=2)).then_inc(o_ready, 1)
                    dve.wait_ge(o_ready, l * 4 + s - 4 * BA + 1)
                    for t in range(TILES):
                        r = dve.tensor_tensor_reduce(out=junk[:, t, :], in0=o[:, t, w], in1=o[:, t, w], scale=1.0, scalar=0.0,
                                                     op0=ALU.mult, op1=ALU.add, accum_out=a_sumsq[:, t, s - 4 * BA:s - 4 * BA + 1])
                    r.then_inc(a_squared, 1)

                def values_to_lo(s):
                    for m in range(2):
                        dve.wait_ge(pT_hi, n_probs_turned(l, s, m))
                        dve.tensor_tensor(pTl[:, m, :, :], bank[4 + m][:, :].rearrange("p (a b) -> p a b", a=2),
                                          pTh[:, m, :, :].bitcast(F32), ALU.subtract).then_inc(pT_split, 1)
                    dve.wait_ge(v_hi, l * 8 + s + 1)
                    dve.tensor_tensor(map_columns(vl[:, :, :]), v_of_pair(s), map_columns(vh[:, :, :].bitcast(F32)),
                                      ALU.subtract).then_inc(v_split, 1)

                for j in range(len(MIX) + 4):
                    u = U_MIX + j
                    kind, b, n, a = MIX[j] if j < len(MIX) else ("wo", 0, 0, 0)
                    if j == PAIRS + 2:
                        dve.wait_ge(a_rstd_ready, l + 1)
                        oa = o[:, :, :].rearrange("p t (a b) -> p (t a) b", b=P)
                        dve.tensor_tensor(oa, oa, bcast(a_rstd[:, :], P), ALU.mult).then_inc(a_normed, 1)
                    if kind == "br":
                        add_branch(b, n, u)
                    if j < PAIRS:
                        add_bias(j)
                    if j < PAIRS - 1:
                        pair_to_lo(j + 1)
                    if 10 <= j < PAIRS + 2:
                        read_values(j - 2)
                    if j == PAIRS + 1:
                        dve.wait_ge(a_squared, l * 4 + 4)
                        dve.tensor_scalar(a_meansq[:, :], a_sumsq[:, :, :].rearrange("p a b -> p (a b)"), 1.0 / P, EPS, ALU.mult,
                                          ALU.add).then_inc(a_mean, 1)
                    if 1 <= j <= 8:
                        values_to_lo(j - 1)
                    if j >= PAIRS:
                        split_o(j)
                    if j == len(MIX):
                        split_quarter(l, 2, 2)
                        split_quarter(l, 2, 3)
                    if j == len(MIX) + 2:
                        scale_quarter(l, 3, 0)
                        split_quarter(l, 3, 0)
                    due = split_at(u) if j < len(MIX) + 3 else []
                    for w in due[:1]:
                        to_lo(l, w)
                    if j < PAIRS:
                        dve.wait_ge(exp_done, l * 24 + 2 * j + 2)
                        dve.reciprocal(rden[j % 2][:, :, :], den[:, :, :]).then_inc(rden_ready, 1)
                        r = rden[j % 2]
                        if j < 8:
                            dve.wait_ge(rden_ready, l * 12 + j + 1)
                            for m in range(2):
                                for t in range(TILES):
                                    w = dve.tensor_scalar(probs[:, m, t, :], probs[:, m, t, :], r[:, m, t:t + 1], None, ALU.mult)
                                w.then_inc(normed, 1)
                        else:
                            dve.wait_ge(rden_ready, l * 12 + j + 1)
                            dve.tensor_scalar(lrden[:, :], r[:, 1, :], mixp[:, 1:2], None, ALU.mult)
                            for t in range(TILES):
                                w = dve.tensor_scalar(probs[:, 0, t, :], probs[:, 0, t, :], r[:, 0, t:t + 1], None, ALU.mult)
                            w.then_inc(a_premix, 1)
                            dve.wait_ge(a_premix, l * 4 + (j - 8) + 1)
                            for t in range(TILES):
                                w = dve.scalar_tensor_tensor(out=probs[:, 0, t, :], in0=probs[:, 1, t, :], scalar=lrden[:, t:t + 1],
                                                             in1=probs[:, 0, t, :], op0=ALU.mult, op1=ALU.add)
                            w.then_inc(mixed, 1)
                        split_o(j)
                    for w in due[1:]:
                        to_lo(l, w)
                    if j == len(MIX) + 1:
                        dve.wait_ge(half_done, n_unit(l, u))
                        residual(0)
                        dve.wait_ge(unit_used, n_unit(l, u) + CREDIT)
                        residual(1)
                    if j == len(MIX) + 3:
                        dve.wait_ge(half_done, n_unit(l, u))
                        residual(2)
                        scale_quarter(l, 3, 1)
                        split_quarter(l, 3, 1)
                        dve.wait_ge(unit_used, n_unit(l, u) + CREDIT)
                        residual(3)
                later_quarters(l, 3, 2, U_FFN2 + 2)
                ffn(l, 1, U_FFN2, NEXT)
            dve.wait_ge(gfin_landed, 16)
            dve.wait_ge(quarter_ready, n_quarter(DEPTH, 0, 3))
            dve.tensor_tensor(gate[:, 1, 0, :], x[:, 1, :], gate[:, 0, 0, :], ALU.mult).then_inc(x_times_g, 1)
            mean_squares(DEPTH, 0)
            dve.wait_ge(rstd_ready, n_norm(DEPTH, 0))
            dve.scalar_tensor_tensor(out=nat[:, 0:2, :].rearrange("p a b -> p (a b)"), in0=x[:, 0, :], scalar=rstd[:, 0, 0:1],
                                     in1=gate[:, 0, 0, :], op0=ALU.mult, op1=ALU.mult).then_inc(out_ready, 1)


def shape_constants():
    import numpy as np
    delta = 255 - np.arange(511)
    n = np.abs(delta)
    large = 8 + (np.log(np.maximum(n, 1).astype(np.float32) / 8) / math.log(1024 / 8) * 8).astype(np.int32)
    bucket = np.where(delta > 0, 16, 0) + np.where(n < 8, n, np.minimum(large, 15))
    onehot = np.zeros((32, 512), np.float32)
    onehot[bucket, np.arange(511)] = 1
    count = (n <= 64).astype(int) + (delta % 4 == 0) + (delta % 16 == 0)
    lncount = np.zeros((T5_HEADS, 512), np.float32)
    lncount[A_HEADS:, :511] = np.where(count > 0, np.log(np.maximum(count, 1)), -BIG)
    col = np.arange(P) % GRID_W
    start = np.clip(col - NA_COLS // 2, 0, GRID_W - NA_COLS)[:, None]
    key_col = (GRID_W - 1 - np.arange(S) % GRID_W)[None]
    mask = np.where((key_col >= start) & (key_col < start + NA_COLS), 0, -BIG).astype(np.float32)
    return np.eye(P, dtype=np.float32), mask, onehot, lncount


def weight_stream(w):
    import numpy as np
    stream = np.empty((DEPTH * UNITS + 2, P, UCOLS), np.float32)
    stream[DEPTH * UNITS:] = 0
    for l in range(DEPTH):
        at = l * UNITS

        def rows(m, a):
            return m[a * 512:(a + 1) * 512].reshape(4, P, 512).transpose(1, 0, 2).reshape(P, UCOLS)

        def ffn(u, w1, w3, w2):
            def up(c, a):
                cols = slice(c * FC, (c + 1) * FC)
                return rows(np.concatenate([w1[:, cols], w3[:, cols]], 1), a)

            def down(c):
                return w2[c * FC:(c + 1) * FC].reshape(2, P, D).transpose(1, 0, 2).reshape(P, UCOLS)

            units = [up(0, 0), up(0, 1)]
            for c in range(1, CHUNKS):
                units += [up(c, 0), up(c, 1), down(c - 1)]
            for k, m in enumerate(units + [down(CHUNKS - 1)]):
                stream[at + u + k] = m

        ffn(U_FFN1, w["w1_ff1"][l], w["w3_ff1"][l], w["w2_ff1"][l])
        ffn(U_FFN2, w["w1_ff2"][l], w["w3_ff2"][l], w["w2_ff2"][l])
        w_in, u = w["w_in"][l], at + U_QKV
        first = {BA: 0, BB: 3 * HEADS_W, BC: 6 * HEADS_W}
        for b in (BC, BB, BA):
            for c in (2, 0, 1):
                for a in range(2):
                    c0 = first[b] + c * HEADS_W
                    stream[u] = rows(w_in[:, c0:c0 + HEADS_W], a)
                    u += 1
        which = {BA: 0, BB: 1, BC: 2}
        for kind, b, n, a in MIX:
            if kind == "gate":
                c0 = 9 * HEADS_W + which[b] * D + n * 512
                stream[u] = rows(w_in[:, c0:c0 + 512], a)
            else:
                stream[u] = rows(w["w_br_" + "abc"[which[b]]][l][:, n * 512:(n + 1) * 512], 0)
            u += 1
        for n in range(2):
            for a in range(2):
                stream[u] = rows(w["w_o"][l][:, n * 512:(n + 1) * 512], a)
                u += 1
    return stream


def kernel(**inputs):
    import numpy as np
    import concourse.bacc as bacc
    from concourse import mybir as mb
    from concourse.bass_utils import run_bass_kernel_spmd

    w = {k: np.asarray(a) for k, a in inputs.items()}
    following = np.roll(w["g_ff1"], -1, 0)
    gains = np.stack([w["g_ff1"], w["g_mix"], w["g_ff2"], following], 1).reshape(DEPTH, 4 * KC, P)
    params = np.concatenate([gains, w["subln_g"][:, None]], 1).transpose(2, 0, 1)
    lam = np.stack([w["lam_q1"], w["lam_k1"], w["lam_q2"], w["lam_k2"]], 1)
    rpb = np.zeros((DEPTH, 2, B_HEADS, TILES, GRID_H, RPB_PITCH), np.float32)
    for half in range(2):
        for t in range(TILES):
            first = GRID_H - 1 - (2 * t + half) + NA_ROWS - 1
            rpb[:, half, :, t, :, 48:48 + 2 * NA_COLS - 1] = w["na_rpb"][:, :, first:first - GRID_H:-1, ::-1]
    eye, mask, onehot, lncount = shape_constants()
    arrays = {"x": w["x"], "stream": weight_stream(w), "params": params, "lam": lam, "g_final": w["g_final"],
              "t5_table": w["t5_table"], "rpb": rpb, "ident": eye, "mask": mask, "onehot": onehot, "lncount": lncount}
    nc = bacc.Bacc("TRN2", target_bir_lowering=False, num_devices=1)
    feed, args = {}, []
    for name, a in arrays.items():
        a = np.ascontiguousarray(a)
        feed["in_" + name] = a
        args.append(nc.dram_tensor("in_" + name, a.shape, mb.dt.from_np(a.dtype), kind="ExternalInput").ap())
    args.append(nc.dram_tensor("out_y", (1, S, D), mb.dt.float32, kind="ExternalOutput").ap())
    build(nc, *args)
    r = run_bass_kernel_spmd(nc, [feed], core_ids=[0])
    return r.results[0]["out_y"]
```
